# Optimizing a Trainium2 kernel written in Bass

```python
import jax, jax.numpy as jnp
from jax import lax
import numpy as np
import math

D_MODEL = 1024
BATCH = 1
SEQ = 256
DEPTH = 2

MLA_HEADS = 4
MLA_Q_LORA = 384
MLA_KV_LORA = 256
MLA_NOPE_DIM = 128
MLA_ROPE_DIM = 64
MLA_V_DIM = 128
MLA_WIDTH = MLA_HEADS * MLA_V_DIM
ROPE_THETA = 10000.0
Q_BLOCK = 128
MLSTM_HEADS = 4
MLSTM_HEAD_DIM = 64
MLSTM_WIDTH = MLSTM_HEADS * MLSTM_HEAD_DIM
MLSTM_CONV = 5
MLSTM_CHUNK = 64
FNET_GROUPS = 4
FNET_GROUP_DIM = 64
FNET_WIDTH = FNET_GROUPS * FNET_GROUP_DIM
MIX_WIDTH = MLA_WIDTH + MLSTM_WIDTH + FNET_WIDTH
IN_SPLITS = (MLA_Q_LORA, MLA_KV_LORA, MLA_ROPE_DIM, MLSTM_WIDTH, MLSTM_WIDTH, MLSTM_WIDTH, 4 * MLSTM_HEADS, FNET_WIDTH)
D_IN = MLA_Q_LORA + MLA_KV_LORA + MLA_ROPE_DIM + 3 * MLSTM_WIDTH + 4 * MLSTM_HEADS + FNET_WIDTH
D_FF = 2816
PLE_DIM = 256
EPS = 1e-6


def rmsnorm(x, g):
    xf = x.astype(jnp.float32)
    y = xf * lax.rsqrt(jnp.mean(xf * xf, axis=-1, keepdims=True) + EPS)
    return (y * g.astype(jnp.float32)).astype(x.dtype)

def swiglu(x, w_gate, w_up, w_down):
    return (jax.nn.silu(x @ w_gate) * (x @ w_up)) @ w_down

def split_cols(z, sizes):
    offs = [int(o) for o in np.cumsum(sizes)[:-1]]
    return jnp.split(z, offs, axis=-1)

def rope_tables(positions):
    inv = 1.0 / (ROPE_THETA ** (jnp.arange(0, MLA_ROPE_DIM, 2, dtype=jnp.float32) / MLA_ROPE_DIM))
    ang = positions.astype(jnp.float32)[..., None] * inv
    return jnp.cos(ang), jnp.sin(ang)

def apply_rope(x, cos, sin):
    xf = x.astype(jnp.float32)
    x1, x2 = jnp.split(xf, 2, axis=-1)
    out = jnp.concatenate([x1 * cos - x2 * sin, x2 * cos + x1 * sin], axis=-1)
    return out.astype(x.dtype)

def mla_mixer(c_q, c_kv, k_rope, cos, sin, q_norm, w_uq, kv_norm, w_ukv):
    B, S, _ = c_q.shape
    q = (rmsnorm(c_q, q_norm) @ w_uq).reshape(B, S, MLA_HEADS, MLA_NOPE_DIM + MLA_ROPE_DIM)
    q_nope, q_rope = q[..., :MLA_NOPE_DIM], q[..., MLA_NOPE_DIM:]
    q_rope = apply_rope(q_rope, cos[:, :, None, :], sin[:, :, None, :])
    kv = (rmsnorm(c_kv, kv_norm) @ w_ukv).reshape(B, S, MLA_HEADS, MLA_NOPE_DIM + MLA_V_DIM)
    k_nope, v = kv[..., :MLA_NOPE_DIM], kv[..., MLA_NOPE_DIM:]
    k_rope = apply_rope(k_rope, cos, sin)
    scale = (MLA_NOPE_DIM + MLA_ROPE_DIM) ** -0.5
    nb = S // Q_BLOCK

    def attend(args):
        qn, qr = args
        s = jnp.einsum('bqhd,bkhd->bhqk', qn, k_nope) + jnp.einsum('bqhr,bkr->bhqk', qr, k_rope)
        pr = jax.nn.softmax(s.astype(jnp.float32) * scale, axis=-1).astype(v.dtype)
        return jnp.einsum('bhqk,bkhd->bqhd', pr, v)

    qn_b = jnp.moveaxis(q_nope.reshape(B, nb, Q_BLOCK, MLA_HEADS, MLA_NOPE_DIM), 1, 0)
    qr_b = jnp.moveaxis(q_rope.reshape(B, nb, Q_BLOCK, MLA_HEADS, MLA_ROPE_DIM), 1, 0)
    o = lax.map(attend, (qn_b, qr_b))
    return jnp.moveaxis(o, 0, 1).reshape(B, S, MLA_WIDTH)

def mlstm_chunkwise(q, k, v, i_pre, f_pre):
    B, H, S, d = q.shape
    L = MLSTM_CHUNK
    nc = S // L
    q = q * d ** -0.5
    lf = jax.nn.log_sigmoid(f_pre)
    causal = jnp.tril(jnp.ones((L, L), dtype=bool))

    def chunks(t):
        return jnp.moveaxis(t.reshape((B, H, nc, L) + t.shape[3:]), 2, 0)

    def step(carry, xs):
        C, n, m = carry
        qc, kc, vc, ic, lfc = xs
        b = jnp.cumsum(lfc, axis=-1)
        D = jnp.where(causal, b[..., :, None] - b[..., None, :] + ic[..., None, :], -jnp.inf)
        m_inter = b + m[..., None]
        m_t = jnp.maximum(m_inter, jnp.max(D, axis=-1))
        w_intra = jnp.exp(D - m_t[..., None])
        w_state = jnp.exp(m_inter - m_t)
        s = jnp.einsum('bhtd,bhsd->bhts', qc, kc) * w_intra
        numer = jnp.einsum('bhts,bhsd->bhtd', s, vc) + w_state[..., None] * jnp.einsum('bhvk,bhtk->bhtv', C, qc)
        denom = jnp.sum(s, axis=-1) + w_state * jnp.einsum('bhk,bhtk->bht', n, qc)
        h = numer / jnp.maximum(jnp.abs(denom), jnp.exp(-m_t))[..., None]
        bL = b[..., -1]
        lw = bL[..., None] - b + ic
        m_new = jnp.maximum(bL + m, jnp.max(lw, axis=-1))
        ws = jnp.exp(lw - m_new[..., None])
        dec = jnp.exp(bL + m - m_new)
        C = dec[..., None, None] * C + jnp.einsum('bhs,bhsv,bhsk->bhvk', ws, vc, kc)
        n = dec[..., None] * n + jnp.einsum('bhs,bhsk->bhk', ws, kc)
        return (C, n, m_new), h

    init = (jnp.zeros((B, H, d, d), jnp.float32), jnp.zeros((B, H, d), jnp.float32), jnp.zeros((B, H), jnp.float32))
    _, h = lax.scan(step, init, (chunks(q), chunks(k), chunks(v), chunks(i_pre), chunks(lf)))
    return jnp.moveaxis(h, 0, 2).reshape(B, H, S, d)

def mlstm_mixer(m_x, m_v, m_o, m_if, conv_w, conv_b, w_q, w_k, i_bias, f_bias, head_norm, skip):
    B, S, _ = m_x.shape
    pad = MLSTM_CONV // 2
    xc = lax.conv_general_dilated(m_x, conv_w[:, None, :], window_strides=(1,), padding=[(pad, pad)],
                                  dimension_numbers=('NWC', 'WIO', 'NWC'), feature_group_count=MLSTM_WIDTH)
    xc = jax.nn.silu(xc + conv_b)
    xh = xc.reshape(B, S, MLSTM_HEADS, MLSTM_HEAD_DIM)
    q = jnp.einsum('bshd,hde->bhse', xh, w_q).astype(jnp.float32)
    k = jnp.einsum('bshd,hde->bhse', xh, w_k).astype(jnp.float32)
    v = m_v.reshape(B, S, MLSTM_HEADS, MLSTM_HEAD_DIM).transpose(0, 2, 1, 3).astype(jnp.float32)
    g = m_if.astype(jnp.float32).reshape(B, S, 2, 2, MLSTM_HEADS)
    i_pre = jnp.transpose(g[:, :, 0] + i_bias.astype(jnp.float32), (2, 0, 3, 1))
    f_pre = jnp.transpose(g[:, :, 1] + f_bias.astype(jnp.float32), (2, 0, 3, 1))
    h_fwd = mlstm_chunkwise(q, k, v, i_pre[0], f_pre[0])
    flip = lambda t: jnp.flip(t, axis=2)
    h_bwd = flip(mlstm_chunkwise(flip(q), flip(k), flip(v), flip(i_pre[1]), flip(f_pre[1])))
    h = (h_fwd + h_bwd).transpose(0, 2, 1, 3)
    h = h * lax.rsqrt(jnp.mean(h * h, axis=-1, keepdims=True) + EPS)
    h = h.reshape(B, S, MLSTM_WIDTH) * head_norm.astype(jnp.float32)
    out = (h + skip.astype(jnp.float32) * xc.astype(jnp.float32)) * jax.nn.sigmoid(m_o.astype(jnp.float32))
    return out.astype(m_x.dtype)

def fnet_mixer(z, w, b):
    B, S, _ = z.shape
    zg = z.reshape(B, S, FNET_GROUPS, FNET_GROUP_DIM).astype(jnp.float32)
    y = jnp.fft.fftn(zg, axes=(1, 3), norm='ortho').real.astype(z.dtype)
    return jnp.einsum('bsgc,gce->bsge', y, w).reshape(B, S, FNET_WIDTH) + b

def first_inputs(seed: int = 0) -> dict:
    key = jax.random.key(seed)
    ks = iter(jax.random.split(key, 40))
    f32 = jnp.float32

    def nrm(shape, fan_in):
        return jax.random.normal(next(ks), shape, f32) * fan_in ** -0.5

    def gain(shape):
        return 1.0 + 0.02 * jax.random.normal(next(ks), shape, f32)

    Ld = DEPTH
    x = jax.random.normal(next(ks), (BATCH, SEQ, D_MODEL), f32)
    p = jax.random.normal(next(ks), (DEPTH, BATCH, SEQ, PLE_DIM), f32)
    offsets = jax.random.randint(next(ks), (BATCH, 1), 0, 4096, dtype=jnp.int32)
    positions = offsets + jnp.arange(SEQ, dtype=jnp.int32)[None, :]
    f_lin = jnp.linspace(3.0, 6.0, MLSTM_HEADS, dtype=f32)
    return {
        'x': x,
        'p': p,
        'positions': positions,
        'ffn1_norm': gain((Ld, D_MODEL)),
        'ffn1_w_gate': nrm((Ld, D_MODEL, D_FF), D_MODEL),
        'ffn1_w_up': nrm((Ld, D_MODEL, D_FF), D_MODEL),
        'ffn1_w_down': nrm((Ld, D_FF, D_MODEL), D_FF),
        'mix_norm': gain((Ld, D_MODEL)),
        'w_in': nrm((Ld, D_MODEL, D_IN), D_MODEL),
        'mla_q_norm': gain((Ld, MLA_Q_LORA)),
        'mla_w_uq': nrm((Ld, MLA_Q_LORA, MLA_HEADS * (MLA_NOPE_DIM + MLA_ROPE_DIM)), MLA_Q_LORA),
        'mla_kv_norm': gain((Ld, MLA_KV_LORA)),
        'mla_w_ukv': nrm((Ld, MLA_KV_LORA, MLA_HEADS * (MLA_NOPE_DIM + MLA_V_DIM)), MLA_KV_LORA),
        'mlstm_conv_w': nrm((Ld, MLSTM_CONV, MLSTM_WIDTH), MLSTM_CONV),
        'mlstm_conv_b': 0.02 * jax.random.normal(next(ks), (Ld, MLSTM_WIDTH), f32),
        'mlstm_w_q': nrm((Ld, MLSTM_HEADS, MLSTM_HEAD_DIM, MLSTM_HEAD_DIM), MLSTM_HEAD_DIM),
        'mlstm_w_k': nrm((Ld, MLSTM_HEADS, MLSTM_HEAD_DIM, MLSTM_HEAD_DIM), MLSTM_HEAD_DIM),
        'mlstm_i_bias': 0.1 * jax.random.normal(next(ks), (Ld, 2, MLSTM_HEADS), f32),
        'mlstm_f_bias': f_lin + 0.1 * jax.random.normal(next(ks), (Ld, 2, MLSTM_HEADS), f32),
        'mlstm_head_norm': gain((Ld, MLSTM_WIDTH)),
        'mlstm_skip': gain((Ld, MLSTM_WIDTH)),
        'fnet_w': nrm((Ld, FNET_GROUPS, FNET_GROUP_DIM, FNET_GROUP_DIM), FNET_GROUP_DIM),
        'fnet_b': 0.02 * jax.random.normal(next(ks), (Ld, FNET_WIDTH), f32),
        'w_out': nrm((Ld, MIX_WIDTH, D_MODEL), MIX_WIDTH),
        'ffn2_norm': gain((Ld, D_MODEL)),
        'ffn2_w_gate': nrm((Ld, D_MODEL, D_FF), D_MODEL),
        'ffn2_w_up': nrm((Ld, D_MODEL, D_FF), D_MODEL),
        'ffn2_w_down': nrm((Ld, D_FF, D_MODEL), D_FF),
        'ple_gate_norm': gain((Ld, D_MODEL)),
        'ple_w_gate': nrm((Ld, D_MODEL, D_MODEL), D_MODEL),
        'ple_w_proj': nrm((Ld, PLE_DIM, D_MODEL), PLE_DIM),
        'ple_post_norm': gain((Ld, D_MODEL)),
        'final_norm': gain((D_MODEL,)),
    }

def first_block(x, p, positions, ffn1_norm, ffn1_w_gate, ffn1_w_up, ffn1_w_down, mix_norm, w_in,
              mla_q_norm, mla_w_uq, mla_kv_norm, mla_w_ukv, mlstm_conv_w, mlstm_conv_b, mlstm_w_q, mlstm_w_k,
              mlstm_i_bias, mlstm_f_bias, mlstm_head_norm, mlstm_skip, fnet_w, fnet_b, w_out,
              ffn2_norm, ffn2_w_gate, ffn2_w_up, ffn2_w_down, ple_gate_norm, ple_w_gate, ple_w_proj,
              ple_post_norm, final_norm):
    cos, sin = rope_tables(positions)
    h = x
    for i in range(DEPTH):
        h = h + 0.5 * swiglu(rmsnorm(h, ffn1_norm[i]), ffn1_w_gate[i], ffn1_w_up[i], ffn1_w_down[i])
        u = rmsnorm(h, mix_norm[i]) @ w_in[i]
        c_q, c_kv, k_rope, m_x, m_v, m_o, m_if, f_in = split_cols(u, IN_SPLITS)
        y_mla = mla_mixer(c_q, c_kv, k_rope, cos, sin, mla_q_norm[i], mla_w_uq[i], mla_kv_norm[i], mla_w_ukv[i])
        y_mlstm = mlstm_mixer(m_x, m_v, m_o, m_if, mlstm_conv_w[i], mlstm_conv_b[i], mlstm_w_q[i], mlstm_w_k[i],
                              mlstm_i_bias[i], mlstm_f_bias[i], mlstm_head_norm[i], mlstm_skip[i])
        y_fnet = fnet_mixer(f_in, fnet_w[i], fnet_b[i])
        y = jnp.concatenate([y_mla, y_mlstm, y_fnet], axis=-1)
        h = h + y @ w_out[i]
        h = h + 0.5 * swiglu(rmsnorm(h, ffn2_norm[i]), ffn2_w_gate[i], ffn2_w_up[i], ffn2_w_down[i])
        e = rmsnorm(p[i] @ ple_w_proj[i], ple_post_norm[i])
        gate = jax.nn.sigmoid(rmsnorm(h, ple_gate_norm[i]) @ ple_w_gate[i])
        h = h + gate * e
    return rmsnorm(h, final_norm)


GRID_W = 64
CTX_LEN = 256
N_MIXERS = 3
N_MOD = 9
FFN_HIDDEN = 256 * ((8 * D_MODEL + 767) // 768)
FFN_RESIDUAL = 0.5
DN_HEAD_DIM = 128
DN_HEADS = D_MODEL // DN_HEAD_DIM
DN_CONV = 5
DN_CHUNK = 64
SWA_HEAD_DIM = 64
SWA_HEADS = D_MODEL // SWA_HEAD_DIM
SWA_KV_HEADS = SWA_HEADS // 4
WINDOW = 128
ATTN_BLOCK = 128
RET_HEADS = 4
RET_QK_DIM = D_MODEL // RET_HEADS
RET_V_DIM = 2 * RET_QK_DIM
RET_CHUNK = 128
ROPE_BASE = 10000.0


def _rms_norm(x, gain):
    xf = x.astype(jnp.float32)
    y = xf * lax.rsqrt(jnp.mean(xf * xf, axis=-1, keepdims=True) + EPS)
    return (y * gain.astype(jnp.float32)).astype(x.dtype)

def _head_group_norm(x, gain):
    xf = x.astype(jnp.float32)
    mu = jnp.mean(xf, axis=-1, keepdims=True)
    var = jnp.mean(jnp.square(xf - mu), axis=-1, keepdims=True)
    return ((xf - mu) * lax.rsqrt(var + EPS) * gain.astype(jnp.float32)).astype(x.dtype)

def _l2_normalize(x):
    xf = x.astype(jnp.float32)
    return (xf * lax.rsqrt(jnp.sum(xf * xf, axis=-1, keepdims=True) + EPS)).astype(x.dtype)

def _modulated_norm(h, gain, shift, scale):
    return _rms_norm(h, gain) * (1.0 + scale) + shift

def _swiglu(h, w1, w2):
    a, b = jnp.split(h @ w1, 2, axis=-1)
    return (jax.nn.silu(a) * b) @ w2

def _rotary_tables(positions, n_freq):
    inv = ROPE_BASE ** (-jnp.arange(n_freq, dtype=jnp.float32) / n_freq)
    ang = jnp.concatenate([p.astype(jnp.float32)[:, None] * inv[None, :] for p in positions], axis=-1)
    return jnp.cos(ang), jnp.sin(ang)

def _rope(x, cos, sin):
    x1, x2 = jnp.split(x, 2, axis=-1)
    c = cos[:, None, :].astype(x.dtype)
    s = sin[:, None, :].astype(x.dtype)
    return jnp.concatenate([x1 * c - x2 * s, x1 * s + x2 * c], axis=-1)

def _short_conv(x, w):
    k = w.shape[0]
    return lax.conv_general_dilated(x, w[:, None, :], window_strides=(1,), padding=[(k // 2, k // 2)],
                                    dimension_numbers=('NWC', 'WIO', 'NWC'), feature_group_count=x.shape[-1])

def _join(a_ctx, a_lat, reverse):
    if reverse:
        a_ctx, a_lat = jnp.flip(a_ctx, 1), jnp.flip(a_lat, 1)
    return jnp.concatenate([a_ctx, a_lat], axis=1)

def _both_dirs(a_ctx, a_lat):
    return jnp.concatenate([_join(a_ctx, a_lat, False), _join(a_ctx, a_lat, True)], axis=0)

def _split_dirs(o, n_batch, ctx_len):
    of, ob = o[:n_batch], o[n_batch:]
    return (of[:, :ctx_len], of[:, ctx_len:], jnp.flip(ob[:, :ctx_len], 1), jnp.flip(ob[:, ctx_len:], 1))

def _to_chunks(a, size):
    n, t, h = a.shape[:3]
    a = a.astype(jnp.float32).reshape((n, t // size, size, h) + a.shape[3:])
    return jnp.moveaxis(a, 3, 1)

def _from_chunks(a):
    n, h, nc, c = a.shape[:4]
    return jnp.moveaxis(a, 1, 3).reshape((n, nc * c, h) + a.shape[4:])

def _gated_delta_chunked(q, k, v, g, beta):
    out_dtype = v.dtype
    n, t, h, dk = q.shape
    dv = v.shape[-1]
    q = _to_chunks(q, DN_CHUNK) * dk ** -0.5
    k = _to_chunks(k, DN_CHUNK)
    v = _to_chunks(v, DN_CHUNK)
    gc = jnp.cumsum(_to_chunks(g, DN_CHUNK), axis=-1)
    beta = _to_chunks(beta, DN_CHUNK)
    causal = jnp.tril(jnp.ones((DN_CHUNK, DN_CHUNK), bool))
    strict = jnp.tril(jnp.ones((DN_CHUNK, DN_CHUNK), bool), -1)
    decay = jnp.exp(jnp.where(causal, gc[..., :, None] - gc[..., None, :], -jnp.inf))
    kb = k * beta[..., None]
    lower = jnp.where(strict, jnp.einsum('nhcid,nhcjd->nhcij', kb, k) * decay, 0.0)
    rhs = jnp.concatenate([v * beta[..., None], kb * jnp.exp(gc)[..., None]], axis=-1)
    uw = lax.linalg.triangular_solve(lower, rhs, left_side=True, lower=True, unit_diagonal=True)
    u, w = uw[..., :dv], uw[..., dv:]
    qk = jnp.einsum('nhcid,nhcjd->nhcij', q, k) * decay
    qg = q * jnp.exp(gc)[..., None]
    g_last = gc[..., -1]
    kd = k * jnp.exp(g_last[..., None] - gc)[..., None]
    xs = tuple(jnp.moveaxis(a, 2, 0) for a in (u, w, qk, qg, kd, jnp.exp(g_last)))

    def step(state, inp):
        u_c, w_c, qk_c, qg_c, kd_c, a_c = inp
        v_new = u_c - jnp.einsum('nhik,nhkv->nhiv', w_c, state)
        o = jnp.einsum('nhik,nhkv->nhiv', qg_c, state) + jnp.einsum('nhij,nhjv->nhiv', qk_c, v_new)
        state = state * a_c[..., None, None] + jnp.einsum('nhjk,nhjv->nhkv', kd_c, v_new)
        return state, o

    _, o = lax.scan(step, jnp.zeros((n, h, dk, dv), jnp.float32), xs)
    return _from_chunks(jnp.moveaxis(o, 0, 2)).astype(out_dtype)

def _retention_log_decay():
    return jnp.log1p(-jnp.exp2(-5.0 - jnp.arange(RET_HEADS, dtype=jnp.float32)))

def _retention_chunked(q, k, v, log_gamma):
    out_dtype = v.dtype
    n, t, h, dk = q.shape
    dv = v.shape[-1]
    q = _to_chunks(q, RET_CHUNK)
    k = _to_chunks(k, RET_CHUNK) * dk ** -0.5
    v = _to_chunks(v, RET_CHUNK)
    pos = jnp.arange(RET_CHUNK, dtype=jnp.float32)
    lg = log_gamma[:, None]
    rel = pos[:, None] - pos[None, :]
    decay = jnp.exp(jnp.where(rel >= 0, lg[:, :, None] * rel, -jnp.inf))
    scores = jnp.einsum('nhcid,nhcjd->nhcij', q, k) * decay[:, None]
    o_intra = jnp.einsum('nhcij,nhcje->nhcie', scores, v)
    q_in = q * jnp.exp(lg * (pos + 1.0))[:, None, :, None]
    k_st = k * jnp.exp(lg * (RET_CHUNK - 1.0 - pos))[:, None, :, None]
    chunk_decay = jnp.exp(lg * RET_CHUNK)[:, :, None]

    def step(state, inp):
        q_c, k_c, v_c = inp
        o = jnp.einsum('nhid,nhde->nhie', q_c, state)
        state = state * chunk_decay + jnp.einsum('nhjd,nhje->nhde', k_c, v_c)
        return state, o

    xs = tuple(jnp.moveaxis(a, 2, 0) for a in (q_in, k_st, v))
    _, o_inter = lax.scan(step, jnp.zeros((n, h, dk, dv), jnp.float32), xs)
    return _from_chunks(o_intra + jnp.moveaxis(o_inter, 0, 2)).astype(out_dtype)

def _sink_softmax(logits, sink):
    sink_col = jnp.broadcast_to(sink.astype(jnp.float32)[None, :, :, None, None], logits.shape[:-1] + (1,))
    return jax.nn.softmax(jnp.concatenate([sink_col, logits], axis=-1), axis=-1)[..., 1:]

def _deltanet_mixer(hc, hx, w_in, conv_w, a_log, dt_bias, o_gain, w_out):
    n_batch, ctx_len = hx.shape[0], hc.shape[1]
    qkv_w = 3 * DN_HEADS * DN_HEAD_DIM
    z_w = DN_HEADS * DN_HEAD_DIM

    def project(h):
        n = h.shape[1]
        qkv, z, ab = jnp.split(h @ w_in, [qkv_w, qkv_w + z_w], axis=-1)
        qkv = jax.nn.silu(_short_conv(qkv, conv_w))
        q, k, v = [a.reshape(n_batch, n, DN_HEADS, DN_HEAD_DIM) for a in jnp.split(qkv, 3, axis=-1)]
        ab = ab.astype(jnp.float32).reshape(n_batch, n, 2, 2, DN_HEADS)
        g = -jnp.exp(a_log.astype(jnp.float32)) * jax.nn.softplus(ab[:, :, :, 0] + dt_bias.astype(jnp.float32))
        beta = jax.nn.sigmoid(ab[:, :, :, 1])
        return _l2_normalize(q), _l2_normalize(k), v, z.reshape(n_batch, n, DN_HEADS, DN_HEAD_DIM), g, beta

    qc, kc, vc, zc, gc, bc = project(hc)
    qx, kx, vx, zx, gx, bx = project(hx)
    g_all = jnp.concatenate([_join(gc[:, :, 0], gx[:, :, 0], False), _join(gc[:, :, 1], gx[:, :, 1], True)], axis=0)
    b_all = jnp.concatenate([_join(bc[:, :, 0], bx[:, :, 0], False), _join(bc[:, :, 1], bx[:, :, 1], True)], axis=0)
    o = _gated_delta_chunked(_both_dirs(qc, qx), _both_dirs(kc, kx), _both_dirs(vc, vx), g_all, b_all)
    ofc, ofx, obc, obx = _split_dirs(o, n_batch, ctx_len)

    def finish(o_f, o_b, z):
        y = _rms_norm(o_f + o_b, o_gain) * jax.nn.silu(z)
        return y.reshape(y.shape[0], y.shape[1], -1) @ w_out

    return finish(ofc, obc, zc), finish(ofx, obx, zx)

def _window_attention_mixer(hc, hx, w_qkv, q_gain, k_gain, sink, w_out, cos, sin):
    n_batch, n_tok = hx.shape[0], hx.shape[1]
    ctx_len = hc.shape[1]
    group = SWA_HEADS // SWA_KV_HEADS
    q_w = SWA_HEADS * SWA_HEAD_DIM
    kv_w = SWA_KV_HEADS * SWA_HEAD_DIM
    scale = SWA_HEAD_DIM ** -0.5
    sink_hg = sink.reshape(SWA_KV_HEADS, group)

    def project(h, rotate):
        n = h.shape[1]
        q, k, v = jnp.split(h @ w_qkv, [q_w, q_w + kv_w], axis=-1)
        q = _rms_norm(q.reshape(n_batch, n, SWA_HEADS, SWA_HEAD_DIM), q_gain)
        k = _rms_norm(k.reshape(n_batch, n, SWA_KV_HEADS, SWA_HEAD_DIM), k_gain)
        if rotate:
            q, k = _rope(q, cos, sin), _rope(k, cos, sin)
        q = (q * scale).reshape(n_batch, n, SWA_KV_HEADS, group, SWA_HEAD_DIM)
        return q, k, v.reshape(n_batch, n, SWA_KV_HEADS, SWA_HEAD_DIM)

    qc, kc, vc = project(hc, False)
    qx, kx, vx = project(hx, True)

    s_c = jnp.einsum('bqhgd,bkhd->bhgqk', qc, kc).astype(jnp.float32)
    p_c = _sink_softmax(s_c, sink_hg).astype(vc.dtype)
    oc = jnp.einsum('bhgqk,bkhd->bqhgd', p_c, vc).reshape(n_batch, ctx_len, q_w)

    span = ATTN_BLOCK + 2 * WINDOW
    pad = ((0, 0), (WINDOW, WINDOW), (0, 0), (0, 0))
    kp, vp = jnp.pad(kx, pad), jnp.pad(vx, pad)
    q_off = jnp.arange(ATTN_BLOCK)
    k_off = jnp.arange(span)

    def block(j):
        start = j * ATTN_BLOCK
        qb = lax.dynamic_slice_in_dim(qx, start, ATTN_BLOCK, axis=1)
        kb = lax.dynamic_slice_in_dim(kp, start, span, axis=1)
        vb = lax.dynamic_slice_in_dim(vp, start, span, axis=1)
        t_pos = start + q_off
        s_pos = start - WINDOW + k_off
        allowed = (jnp.abs(t_pos[:, None] - s_pos[None, :]) <= WINDOW) & (s_pos >= 0) & (s_pos < n_tok)
        s_ctx = jnp.einsum('bqhgd,bkhd->bhgqk', qb, kc).astype(jnp.float32)
        s_win = jnp.where(allowed, jnp.einsum('bqhgd,bkhd->bhgqk', qb, kb).astype(jnp.float32), -jnp.inf)
        p = _sink_softmax(jnp.concatenate([s_ctx, s_win], axis=-1), sink_hg).astype(vb.dtype)
        return (jnp.einsum('bhgqk,bkhd->bqhgd', p[..., :ctx_len], vc)
                + jnp.einsum('bhgqk,bkhd->bqhgd', p[..., ctx_len:], vb))

    ox = lax.map(block, jnp.arange(n_tok // ATTN_BLOCK))
    ox = jnp.moveaxis(ox, 0, 1).reshape(n_batch, n_tok, q_w)
    return oc @ w_out, ox @ w_out

def _retention_mixer(hc, hx, w_in, gn_gain, w_out, cos, sin):
    n_batch, ctx_len = hx.shape[0], hc.shape[1]
    qk_w = RET_HEADS * RET_QK_DIM
    v_w = RET_HEADS * RET_V_DIM

    def project(h):
        n = h.shape[1]
        q, k, v, gf, gb = jnp.split(h @ w_in, [qk_w, 2 * qk_w, 2 * qk_w + v_w, 2 * qk_w + 2 * v_w], axis=-1)
        hq = lambda a: a.reshape(n_batch, n, RET_HEADS, RET_QK_DIM)
        hv = lambda a: a.reshape(n_batch, n, RET_HEADS, RET_V_DIM)
        return hq(q), hq(k), hv(v), hv(gf), hv(gb)

    qc, kc, vc, gfc, gbc = project(hc)
    qx, kx, vx, gfx, gbx = project(hx)
    qx, kx = _rope(qx, cos, sin), _rope(kx, cos, sin)
    o = _retention_chunked(_both_dirs(qc, qx), _both_dirs(kc, kx), _both_dirs(vc, vx), _retention_log_decay())
    ofc, ofx, obc, obx = _split_dirs(o, n_batch, ctx_len)
    gain = gn_gain.reshape(2, RET_HEADS, RET_V_DIM)

    def finish(o_f, o_b, g_f, g_b):
        y = (jax.nn.silu(g_f) * _head_group_norm(o_f, gain[0]) + jax.nn.silu(g_b) * _head_group_norm(o_b, gain[1]))
        return y.reshape(y.shape[0], y.shape[1], -1) @ w_out

    return finish(ofc, obc, gfc, gbc), finish(ofx, obx, gfx, gbx)

def second_inputs(seed: int = 0) -> dict:
    key = jax.random.key(seed)
    ks = jax.random.split(key, 24)
    d, f = D_MODEL, FFN_HIDDEN
    n_dn, n_swa, n_ret = (len(range(kind, DEPTH, N_MIXERS)) for kind in range(N_MIXERS))

    def nrm(k, shape, std):
        return std * jax.random.normal(k, shape, jnp.float32)

    dn_in = 4 * DN_HEADS * DN_HEAD_DIM + 4 * DN_HEADS
    swa_in = (SWA_HEADS + 2 * SWA_KV_HEADS) * SWA_HEAD_DIM
    ret_v = RET_HEADS * RET_V_DIM
    ret_in = 2 * RET_HEADS * RET_QK_DIM + 3 * ret_v
    dt = jnp.exp(jax.random.uniform(ks[12], (n_dn, 2, DN_HEADS), jnp.float32, math.log(1e-3), math.log(1e-1)))
    return {
        "x": nrm(ks[0], (BATCH, SEQ, d), 1.0),
        "c": nrm(ks[1], (BATCH, d), 1.0),
        "ctx": nrm(ks[2], (BATCH, CTX_LEN, d), 1.0),
        "c_ctx": nrm(ks[3], (d,), 1.0),
        "ada_w": nrm(ks[4], (DEPTH, d, N_MOD * d), 0.5 * d ** -0.5),
        "ada_b": nrm(ks[5], (DEPTH, N_MOD * d), 0.02),
        "norm_g": 1.0 + nrm(ks[6], (DEPTH, 3, d), 0.02),
        "ffn_w1": nrm(ks[7], (DEPTH, 2, d, 2 * f), d ** -0.5),
        "ffn_w2": nrm(ks[8], (DEPTH, 2, f, d), f ** -0.5),
        "dn_w_in": nrm(ks[9], (n_dn, d, dn_in), d ** -0.5),
        "dn_conv": nrm(ks[10], (n_dn, DN_CONV, 3 * DN_HEADS * DN_HEAD_DIM), DN_CONV ** -0.5),
        "dn_a_log": jnp.log(jax.random.uniform(ks[11], (n_dn, 2, DN_HEADS), jnp.float32, 1.0, 16.0)),
        "dn_dt_bias": dt + jnp.log(-jnp.expm1(-dt)),
        "dn_o_gain": 1.0 + nrm(ks[13], (n_dn, DN_HEAD_DIM), 0.02),
        "dn_w_out": nrm(ks[14], (n_dn, DN_HEADS * DN_HEAD_DIM, d), (DN_HEADS * DN_HEAD_DIM) ** -0.5),
        "swa_w_qkv": nrm(ks[15], (n_swa, d, swa_in), d ** -0.5),
        "swa_q_gain": 1.0 + nrm(ks[16], (n_swa, SWA_HEAD_DIM), 0.02),
        "swa_k_gain": 1.0 + nrm(ks[17], (n_swa, SWA_HEAD_DIM), 0.02),
        "swa_sink": nrm(ks[18], (n_swa, SWA_HEADS), 1.0),
        "swa_w_out": nrm(ks[19], (n_swa, SWA_HEADS * SWA_HEAD_DIM, d), (SWA_HEADS * SWA_HEAD_DIM) ** -0.5),
        "ret_w_in": nrm(ks[20], (n_ret, d, ret_in), d ** -0.5),
        "ret_gn_gain": 1.0 + nrm(ks[21], (n_ret, 2, ret_v), 0.02),
        "ret_w_out": nrm(ks[22], (n_ret, ret_v, d), ret_v ** -0.5),
    }

def second_block(x, c, ctx, c_ctx, ada_w, ada_b, norm_g, ffn_w1, ffn_w2, dn_w_in, dn_conv, dn_a_log, dn_dt_bias,
              dn_o_gain, dn_w_out, swa_w_qkv, swa_q_gain, swa_k_gain, swa_sink, swa_w_out, ret_w_in, ret_gn_gain,
              ret_w_out):
    n_batch, n_tok, d = x.shape
    ROWS = n_tok // GRID_W
    rows = jnp.repeat(jnp.arange(ROWS), GRID_W)
    cols = jnp.tile(jnp.arange(GRID_W), ROWS)
    swa_cos, swa_sin = _rotary_tables((rows, cols), SWA_HEAD_DIM // 4)
    ret_cos, ret_sin = _rotary_tables((jnp.arange(n_tok),), RET_QK_DIM // 2)
    cond_x = jax.nn.silu(c)
    cond_c = jax.nn.silu(c_ctx)

    for i in range(DEPTH):
        kind, slot, last = i % N_MIXERS, i // N_MIXERS, i == DEPTH - 1
        mx = (cond_x @ ada_w[i] + ada_b[i]).reshape(n_batch, 3, 3, 1, d)
        mc = (cond_c @ ada_w[i] + ada_b[i]).reshape(3, 3, d)

        x = x + FFN_RESIDUAL * mx[:, 0, 2] * _swiglu(
            _modulated_norm(x, norm_g[i, 0], mx[:, 0, 0], mx[:, 0, 1]), ffn_w1[i, 0], ffn_w2[i, 0])
        ctx = ctx + FFN_RESIDUAL * mc[0, 2] * _swiglu(
            _modulated_norm(ctx, norm_g[i, 0], mc[0, 0], mc[0, 1]), ffn_w1[i, 0], ffn_w2[i, 0])

        hx = _modulated_norm(x, norm_g[i, 1], mx[:, 1, 0], mx[:, 1, 1])
        hc = _modulated_norm(ctx, norm_g[i, 1], mc[1, 0], mc[1, 1])
        if kind == 0:
            oc, ox = _deltanet_mixer(hc, hx, dn_w_in[slot], dn_conv[slot], dn_a_log[slot], dn_dt_bias[slot],
                                     dn_o_gain[slot], dn_w_out[slot])
        elif kind == 1:
            oc, ox = _window_attention_mixer(hc, hx, swa_w_qkv[slot], swa_q_gain[slot], swa_k_gain[slot],
                                             swa_sink[slot], swa_w_out[slot], swa_cos, swa_sin)
        else:
            oc, ox = _retention_mixer(hc, hx, ret_w_in[slot], ret_gn_gain[slot], ret_w_out[slot], ret_cos, ret_sin)
        x = x + mx[:, 1, 2] * ox

        x = x + FFN_RESIDUAL * mx[:, 2, 2] * _swiglu(
            _modulated_norm(x, norm_g[i, 2], mx[:, 2, 0], mx[:, 2, 1]), ffn_w1[i, 1], ffn_w2[i, 1])
        if not last:
            ctx = ctx + mc[1, 2] * oc
            ctx = ctx + FFN_RESIDUAL * mc[2, 2] * _swiglu(
                _modulated_norm(ctx, norm_g[i, 2], mc[2, 0], mc[2, 1]), ffn_w1[i, 1], ffn_w2[i, 1])
    return x


def setup_inputs(seed=0):
    out = dict(first_inputs(seed))
    for name, value in second_inputs(seed + 1).items():
        if name != "x":
            out[name + "_2"] = value
    return out


def reference(
    x, p, positions, ffn1_norm, ffn1_w_gate, ffn1_w_up, ffn1_w_down, mix_norm, w_in, mla_q_norm,
    mla_w_uq, mla_kv_norm, mla_w_ukv, mlstm_conv_w, mlstm_conv_b, mlstm_w_q, mlstm_w_k,
    mlstm_i_bias, mlstm_f_bias, mlstm_head_norm, mlstm_skip, fnet_w, fnet_b, w_out, ffn2_norm,
    ffn2_w_gate, ffn2_w_up, ffn2_w_down, ple_gate_norm, ple_w_gate, ple_w_proj, ple_post_norm,
    final_norm, c_2, ctx_2, c_ctx_2, ada_w_2, ada_b_2, norm_g_2, ffn_w1_2, ffn_w2_2, dn_w_in_2,
    dn_conv_2, dn_a_log_2, dn_dt_bias_2, dn_o_gain_2, dn_w_out_2, swa_w_qkv_2, swa_q_gain_2,
    swa_k_gain_2, swa_sink_2, swa_w_out_2, ret_w_in_2, ret_gn_gain_2, ret_w_out_2,
):
    x = first_block(
        x, p, positions, ffn1_norm, ffn1_w_gate, ffn1_w_up, ffn1_w_down, mix_norm, w_in,
        mla_q_norm, mla_w_uq, mla_kv_norm, mla_w_ukv, mlstm_conv_w, mlstm_conv_b, mlstm_w_q,
        mlstm_w_k, mlstm_i_bias, mlstm_f_bias, mlstm_head_norm, mlstm_skip, fnet_w, fnet_b,
        w_out, ffn2_norm, ffn2_w_gate, ffn2_w_up, ffn2_w_down, ple_gate_norm, ple_w_gate,
        ple_w_proj, ple_post_norm, final_norm,
    )
    return second_block(
        x, c_2, ctx_2, c_ctx_2, ada_w_2, ada_b_2, norm_g_2, ffn_w1_2, ffn_w2_2, dn_w_in_2,
        dn_conv_2, dn_a_log_2, dn_dt_bias_2, dn_o_gain_2, dn_w_out_2, swa_w_qkv_2, swa_q_gain_2,
        swa_k_gain_2, swa_sink_2, swa_w_out_2, ret_w_in_2, ret_gn_gain_2, ret_w_out_2,
    )


_drawn_inputs = setup_inputs


def setup_inputs(seed=0):
    import zlib

    import numpy as np

    out = dict(_drawn_inputs(seed))
    spreads = {}
    factors = {'ffn1_norm': 4.571,
     'mix_norm': 2.931,
     'mla_q_norm': 8.0,
     'mla_kv_norm': 8.0,
     'mlstm_conv_b': 3.086,
     'mlstm_i_bias': 8.0,
     'mlstm_head_norm': 8.0,
     'mlstm_skip': 8.0,
     'fnet_b': 4.222,
     'ffn2_norm': 5.757,
     'ple_gate_norm': 8.0,
     'ple_post_norm': 4.736,
     'norm_g_2': 6.467,
     'dn_o_gain_2': 8.0,
     'swa_q_gain_2': 21.664,
     'swa_k_gain_2': 8.0,
     'swa_sink_2': 8.0}
    for name, (base, spread) in spreads.items():
        noise = np.random.default_rng([zlib.crc32(name.encode()), seed]).standard_normal(out[name].shape)
        drawn = base * np.exp(spread * noise) if base else spread * noise
        out[name] = __import__('jax').numpy.asarray(drawn.astype(out[name].dtype))
    for name, factor in factors.items():
        out[name] = (out[name] * factor).astype(out[name].dtype)
    return out
```

```python
from contextlib import ExitStack

import numpy as np
import concourse.bass as bass
from concourse import mybir

ALU = mybir.AluOpType
ACT = mybir.ActivationFunctionType
F32 = mybir.dt.float32
F32R = mybir.dt.float32r
I32 = mybir.dt.int32
AX = mybir.AxisListType.X

P = 128
D = 1024
KT = D // P
TOK = 256
LAYERS = 2
FF = 2816
FT = FF // P
CHUNK = 2048
SLOTS = 4
EPS = 1e-6
HEADS = 4
Q_LORA, KV_LORA, NOPE, ROPE, VDIM = 384, 256, 128, 64, 128
MLA_SCALE = (NOPE + ROPE) ** -0.5
LH = 64
DN_HEADS = 8
DN_GROUP = 4
DN_CONV = 5
SWA_HEADS, SWA_KV, SWA_DIM, WINDOW = 16, 4, 64, 128
NEG = -1e30
TWO_PI = 2 * np.pi
MASK = NEG



def by_partition(v):
    return np.ascontiguousarray(v.reshape(-1, P).T)


def columns(w, cols):
    picked = w[:, cols]
    return picked.reshape(w.shape[0] // P, P, -1).transpose(1, 0, 2).reshape(P, -1)


def block_diagonal(a, b):
    out = np.zeros((P, P), np.float32)
    out[:LH, :LH] = a
    out[LH:, LH:] = b
    return out


def split_points():
    sizes = dict(c_q=Q_LORA, c_kv=KV_LORA, k_rope=ROPE, m_x=256, m_v=256, m_o=256, m_if=16, f_in=256)
    at, out = 0, {}
    for name, n in sizes.items():
        out[name] = at
        at += n
    return out


def vector_table():
    table, at = {}, 0
    def add(name, width):
        nonlocal at
        table[name] = (at, width)
        at += width
    for l in range(LAYERS):
        for name, width in (("ffn1_norm", 8), ("mix_norm", 8), ("q_norm", 3), ("kv_norm", 2), ("conv_w", 10),
                            ("conv_b", 2), ("i_bias", 2), ("f_bias", 2), ("head_norm", 2), ("skip", 2),
                            ("fnet_b", 2), ("ffn2_norm", 8), ("ple_gate_norm", 8), ("ple_post_norm", 8)):
            add(f"{name}{l}", width)
        add(f"ada_b{l}", 72)
        add(f"norm_g{l}", 24)
    add("final_norm", 8)
    add("inv_freq", 1)
    add("cond", 16)
    add("dn_conv", 24 * DN_CONV)
    add("dn_a_log", 16)
    add("dn_dt_bias", 16)
    add("dn_o_gain", 1)
    add("swa_q_gain", 1)
    add("swa_k_gain", 1)
    add("sink", 32)
    return table, at


def vector_values(a):
    table, width = vector_table()
    out = np.zeros((P, width), np.float32)
    def put(name, value):
        at, n = table[name]
        out[:value.shape[0], at:at + n] = value
    for l in range(LAYERS):
        for name, source in (("ffn1_norm", "ffn1_norm"), ("mix_norm", "mix_norm"), ("q_norm", "mla_q_norm"),
                             ("kv_norm", "mla_kv_norm"), ("conv_b", "mlstm_conv_b"), ("head_norm", "mlstm_head_norm"),
                             ("skip", "mlstm_skip"), ("fnet_b", "fnet_b"), ("ffn2_norm", "ffn2_norm"),
                             ("ple_gate_norm", "ple_gate_norm"), ("ple_post_norm", "ple_post_norm")):
            put(f"{name}{l}", by_partition(a[source][l]))
        put(f"conv_w{l}", a["mlstm_conv_w"][l].reshape(5, 2, P).transpose(2, 1, 0).reshape(P, 10))
        put(f"i_bias{l}", a["mlstm_i_bias"][l].T)
        put(f"f_bias{l}", a["mlstm_f_bias"][l].T)
        put(f"ada_b{l}", by_partition(a["ada_b_2"][l]))
        put(f"norm_g{l}", by_partition(a["norm_g_2"][l].reshape(-1)))
    put("final_norm", by_partition(a["final_norm"]))
    put("inv_freq", inverse_frequencies(P))
    cond = np.stack([by_partition(a["c_2"][0]), by_partition(a["c_ctx_2"])], axis=2)
    put("cond", cond.reshape(P, 16))
    put("dn_conv", a["dn_conv_2"][0].reshape(DN_CONV, 24, P).transpose(2, 1, 0).reshape(P, -1))
    put("dn_a_log", np.broadcast_to(a["dn_a_log_2"][0].reshape(1, 16), (P, 16)))
    put("dn_dt_bias", np.broadcast_to(a["dn_dt_bias_2"][0].reshape(1, 16), (P, 16)))
    put("dn_o_gain", a["dn_o_gain_2"][0].reshape(P, 1))
    put("swa_q_gain", np.concatenate([a["swa_q_gain_2"][0]] * 2).reshape(P, 1))
    put("swa_k_gain", np.concatenate([a["swa_k_gain_2"][0]] * 2).reshape(P, 1))
    order = [h for pair in swa_pairs() for h in pair for _ in range(2)]
    put("sink", np.broadcast_to(a["swa_sink_2"][0][order].reshape(1, 32), (P, 32)))
    return out


def inverse_frequencies(rows):
    f = np.float32(1.0) / np.power(np.float32(10000.0), np.arange(0, ROPE, 2, dtype=np.float32) / np.float32(ROPE))
    return np.tile(f.astype(np.float32), rows // 32).reshape(rows, 1)


def constant_table():
    table, at = {}, 0
    for name, shape in (("identity", (P,)), ("ones", (P,)), ("head_ones", (P,)), ("rotate", (P,)),
                        ("not_before", (2, P)), ("after", (2, P)), ("levels", (7, P)),
                        ("lstm_mask", (2, 2, TOK)), ("select", (HEADS, P)), ("select_pair", (2, P)),
                        ("swa_cos", (TOK,)), ("swa_sin", (TOK,)), ("swa_mask", (2, TOK))):
        table[name] = (at, shape)
        at += int(np.prod(shape))
    return table, at


def constant_values():
    table, width = constant_table()
    out = np.zeros((P, width), np.float32)
    def put(name, value):
        at, shape = table[name]
        out[:value.shape[0], at:at + int(np.prod(shape))] = value.reshape(value.shape[0], -1)
    i, j = np.arange(P)[None, :], np.arange(P)[:, None]
    put("identity", (i == j).astype(np.float32))
    put("ones", np.ones((P, P)))
    put("head_ones", (i // LH == j // LH).astype(np.float32))
    rot = np.zeros((P, P))
    for base in (0, 64):
        for r in range(32):
            rot[base + 32 + r, base + r] = -1.0
            rot[base + r, base + 32 + r] = 1.0
    put("rotate", rot)
    put("not_before", np.stack([i >= j, i <= j], 1).astype(np.float32))
    put("after", np.stack([i > j, i < j], 1).astype(np.float32))
    put("levels", np.stack([(i // (2 << k) == j // (2 << k)) & (i // (1 << k) != j // (1 << k))
                            for k in range(7)], 1).astype(np.float32))
    t = np.arange(TOK)[None, :]
    mask = np.zeros((P, 2, 2, TOK))
    for st in range(2):
        s = st * P + j
        mask[:, 0, st] = np.where(s <= t, 0.0, MASK)
        mask[:, 1, st] = np.where(s >= t, 0.0, MASK)
    put("lstm_mask", mask)
    put("select", (np.arange(HEADS)[:, None, None] == np.arange(HEADS)[None, :, None]) * np.ones((1, 1, P)))
    pair = np.zeros((HEADS, 2, P))
    for h in range(HEADS):
        pair[h, h // 2, (h % 2) * LH:(h % 2) * LH + LH] = 1.0
    put("select_pair", pair)
    inv = np.power(np.float32(10000.0), -np.arange(16, dtype=np.float32) / np.float32(16)).astype(np.float32)
    tok = np.arange(TOK)
    ang = np.concatenate([(tok // 64).astype(np.float32)[:, None] * inv, (tok % 64).astype(np.float32)[:, None] * inv], 1)
    put("swa_cos", np.tile(np.cos(ang).T, (4, 1)))
    put("swa_sin", np.tile(np.sin(ang).T, (4, 1)))
    keep = np.zeros((P, 2, TOK))
    for qt in range(2):
        keep[:, qt] = np.where(np.abs(qt * P + j - t) <= WINDOW, 0.0, MASK)
    put("swa_mask", keep)
    return out


def dft_tables():
    c = np.arange(LH)
    ang = TWO_PI * (np.outer(c, c) % LH) / LH
    channel = np.concatenate([block_diagonal(np.cos(ang) / 8, np.cos(ang) / 8),
                              block_diagonal(np.sin(ang) / 8, np.sin(ang) / 8)], 1)
    s = np.arange(TOK)
    ang = TWO_PI * (np.outer(s, s) % TOK) / TOK
    place = lambda m: m.reshape(2, P, TOK).transpose(1, 0, 2).reshape(P, -1)
    return np.concatenate([channel, place(np.cos(ang) / 16), place(-np.sin(ang) / 16)], 1).astype(np.float32)


def ffn_chunks(gate, up, down):
    for c in range(FT // 2):
        cols = np.arange(c * 256, c * 256 + 256)
        yield columns(gate, cols)
        yield columns(up, cols)
    for c in range(FT // 2):
        yield down[c * 256:c * 256 + 256].reshape(2, P, D).transpose(1, 0, 2).reshape(P, -1)


def dense_chunks(w):
    for c in range(0, w.shape[1], 256):
        yield columns(w, np.arange(c, c + 256))


def mix1_chunks(a, l):
    w, at = a["w_in"][l], split_points()
    run = lambda name, n=256, off=0: np.arange(at[name] + off, at[name] + off + n)
    yield columns(w, run("c_q"))
    yield columns(w, np.concatenate([run("c_q", 128, 256), run("c_kv", 128)]))
    yield columns(w, np.concatenate([run("c_kv", 128, 128), run("k_rope", 64), run("k_rope", 64)]))
    yield columns(w, run("m_x"))
    yield columns(w, run("m_if", 16))
    yield columns(w, run("m_v"))
    yield columns(w, run("m_o"))
    yield columns(w, run("f_in"))
    uq = a["mla_w_uq"][l]
    head = NOPE + ROPE
    yield columns(uq, np.concatenate([np.arange(h * head, h * head + NOPE) for h in range(HEADS)]))
    yield columns(uq, np.concatenate([np.arange(h * head + NOPE, (h + 1) * head) for h in range(HEADS)]))
    yield columns(a["mla_w_ukv"][l], np.arange(1024))
    maps = [block_diagonal(m[2 * p], m[2 * p + 1])
            for m in (a["mlstm_w_q"][l], a["mlstm_w_k"][l], a["fnet_w"][l]) for p in range(2)]
    yield np.concatenate(maps + [dft_tables()], 1)
    yield from dense_chunks(a["w_out"][l])


def ple_chunks(a, l):
    yield columns(np.ascontiguousarray(a["p"][l, 0].T), np.arange(TOK))
    yield columns(a["ple_w_proj"][l], np.arange(D))
    yield from dense_chunks(a["ple_w_gate"][l])


def deltanet_chunks(a):
    w = a["dn_w_in_2"][0]
    yield columns(w, np.arange(4096, 4128))
    for g in range(DN_HEADS // DN_GROUP):
        for part in range(4):
            base = part * D + g * DN_GROUP * P
            yield from dense_chunks(w[:, base:base + DN_GROUP * P])
    yield from dense_chunks(a["dn_w_out_2"][0])


def swa_pairs():
    group = SWA_HEADS // SWA_KV
    return [(2 * g * group + j, (2 * g + 1) * group + j) for g in range(SWA_KV // 2) for j in range(group)]


def swa_chunks(a):
    w = a["swa_w_qkv_2"][0]
    order = np.concatenate([np.arange(h * SWA_DIM, (h + 1) * SWA_DIM) for pair in swa_pairs() for h in pair])
    for c in range(0, D, 256):
        yield columns(w, order[c:c + 256])
    yield columns(w, np.arange(1024, 1280))
    yield columns(w, np.arange(1280, 1536))
    yield from dense_chunks(a["swa_w_out_2"][0][order])


STAGES = [(kind, l) for l in range(LAYERS) for kind in ("ffn1", "mix1", "ffn2", "ple")] + [("final", 0)]
for _l in range(LAYERS):
    STAGES += [("ada", _l), ("ffn_a", _l), ("delta" if _l == 0 else "swa", _l), ("ffn_b", _l)]


def stage_chunks(a, kind, l):
    if kind in ("ffn1", "ffn2"):
        return ffn_chunks(a[f"{kind}_w_gate"][l], a[f"{kind}_w_up"][l], a[f"{kind}_w_down"][l])
    if kind == "mix1":
        return mix1_chunks(a, l)
    if kind == "ple":
        return ple_chunks(a, l)
    if kind == "ada":
        return dense_chunks(a["ada_w_2"][l])
    if kind in ("ffn_a", "ffn_b"):
        n = 0 if kind == "ffn_a" else 1
        w1 = a["ffn_w1_2"][l, n]
        return ffn_chunks(w1[:, :FF], w1[:, FF:], a["ffn_w2_2"][l, n])
    if kind == "delta":
        return deltanet_chunks(a)
    if kind == "swa":
        return swa_chunks(a)
    return ()


def chunk_count(kind):
    return {"ffn1": 33, "ffn2": 33, "ffn_a": 33, "ffn_b": 33, "mix1": 16, "ple": 6, "final": 0, "ada": 36,
            "delta": 1 + 16 + 4, "swa": 10}[kind]


def split_count(kind):
    return chunk_count(kind) if kind.startswith("ffn") else 0



SEMAPHORES = (
    "tables_in",
    "x_in", "ctx_in", "pos_in", "ple_in",
    "weights_used",
    "w_high",
    "split_used",
    "a_high", "x_high",
    "x_split",
    "low_full", "low_free", "high_full", "high_free",
    "act_step", "vec_step", "pool_step",
    "squares",
    "root",
    "final_normed",
    "normed",
    "scaled",
    "residual",
    "rope_angle", "rope_table",
    "latent",
    "rotated",
    "neg_max", "probs", "probs_scaled",
    "conv_out", "conv_act",
    "gate_abs", "gate_ln", "gate_rows", "gate_exp", "decay_in", "decay", "weighted", "out_done",
    "group_ready", "floor_done", "mix_done", "ple_used", "mod_in", "mod_out",
    "shifted",
    "decay_tok", "decay_col", "rate", "pads",
    "dn_act", "dn_normed", "row_decay", "inv_start", "masked", "state_done", "sink_exp",
    "stream_out", "all_done",
)


class Engine:

    def __init__(self, g, engine):
        self.g, self.engine = g, engine
        self.wait_ge = engine.wait_ge
        self.seen, self.made = {}, {}
        self.tiles = {"low": 0, "high": 0}
        self.freed = {"low": 0, "high": 0}
        self.foreign = {"low": False, "high": False}
        self.last_sem = None
        self.chunks = self.splits = 0

    def due(self, name, more=1):
        self.seen[name] = self.seen.get(name, 0) + more
        return self.seen[name]

    def adds(self, name):
        self.made[name] = self.made.get(name, 0) + 1
        self.last_sem, self.last_count = self.g.sem[name], self.made[name]
        return 1

    def frees(self, side):
        self.freed[side] += 1
        self.last_sem, self.last_count = self.g.sem[side + "_free"], self.freed[side]
        return 1

    def tile(self, side, peek=False):
        n = self.tiles[side]
        self.tiles[side] += 1
        if self.foreign[side] and not peek:
            self.foreign[side] = False
            self.wait_ge(self.g.sem[side + "_free"], self.freed[side])
        return self.g.banks[side][n % 4]

    def skip(self, side, n=1):
        self.tiles[side] += n
        self.other_frees(side, n)

    def other_frees(self, side, n=1):
        self.freed[side] += n
        self.foreign[side] = True


class Tensor(Engine):

    def __init__(self, g, engine):
        super().__init__(g, engine)
        self.unreleased = []

    def open(self, side):
        n = self.tiles[side]
        self.tiles[side] += 1
        return self.g.banks[side][n % 4]

    def chunk(self, *shape):
        self.chunks += 1
        return self.g.slot(self.chunks - 1, *shape)

    def release(self, name="weights_used"):
        self.unreleased.append(name)

    def mm(self, out, lhsT, rhs, start=True, stop=True, full=None):
        ins = self.g.nc.tensor.matmul(out, lhsT, rhs, start=start, stop=stop)
        if full:
            ins.then_inc(self.g.sem[full + "_full"], 1)
        elif self.unreleased:
            ins.then_inc(self.g.sem[self.unreleased.pop(0)], 1)

    def transpose(self, out, in_, full=None):
        n = in_.shape[0]
        ins = self.g.nc.tensor.transpose(out, in_, self.g.const("identity")[0:n, 0:n])
        if full:
            ins.then_inc(self.g.sem[full + "_full"], 1)
        elif self.unreleased:
            ins.then_inc(self.g.sem[self.unreleased.pop(0)], 1)


class Shared:

    def __init__(self, nc, ctx, args):
        self.nc, self.args = nc, args
        self.sem = {n: ctx.enter_context(nc.semaphore("s_" + n)) for n in SEMAPHORES}
        self.landed = [ctx.enter_context(nc.semaphore(f"s_landed{i}")) for i in range(SLOTS)]
        def sb(name, shape, dtype=F32):
            return ctx.enter_context(nc.sbuf_tensor("sb_" + name, shape, dtype))
        self.ring = sb("ring", [P, SLOTS, CHUNK])
        self.vec_table, n = vector_table()
        self.vectors = sb("vectors", [P, n])
        self.const_at, n = constant_table()
        self.consts = sb("consts", [P, n])
        self.h = sb("h", [P, KT, 2 * TOK])
        self.root = sb("root", [P, 2 * TOK])
        self.rinv = sb("rinv", [P, 2 * TOK])
        self.silu = sb("silu", [P, 2, 2 * TOK])
        self.eps = sb("eps", [P, 1])
        self.rope = sb("rope", [P, 2, TOK])
        self.mod = sb("mod", [P, 9, KT, 2])
        self.cond = sb("cond_act", [P, KT, 2])
        with ExitStack() as mixers:
            def sb_mixers(name, shape):
                return mixers.enter_context(nc.sbuf_tensor("sb_" + name, shape, F32))
            self.xn = sb_mixers("xn", [P, KT, 2 * TOK])
            self.sq = sb_mixers("sq", [P, KT, 2 * TOK])
            self.arena = sb_mixers("arena", [P, ARENA])
        self.x_split = sb("x_split", [P, 2, KT, 2 * TOK], F32R)
        self.inner_space = sb("inner_space", [P, FT * 2 * TOK])
        self.w_split = sb("w_split", [P, 2, 2, CHUNK], F32R)
        self.a_split = sb("a_split", [P, 2, 2, 2, 2 * TOK], F32R)
        self.rest = sb("rest", [P, ARENA - FT * 2 * TOK - 4 * CHUNK - 8 * 2 * TOK])
        self.banks = {s: [ctx.enter_context(nc.psum_tensor(f"ps_{s}{i}", [P, 512], F32)) for i in range(4)]
                      for s in ("low", "high")}

    def slot(self, n, *shape):
        size = int(np.prod(shape))
        flat = self.ring[:, n % SLOTS, 0:size]
        if len(shape) == 2:
            return flat.rearrange("p (a b) -> p a b", a=shape[0])
        return flat

    def vec(self, name):
        at, n = self.vec_table[name]
        return self.vectors[:, at:at + n]

    def const(self, name):
        at, shape = self.const_at[name]
        flat = self.consts[:, at:at + int(np.prod(shape))]
        if len(shape) == 2:
            return flat.rearrange("p (a b) -> p a b", a=shape[0])
        if len(shape) == 3:
            return flat.rearrange("p (a b c) -> p a b c", a=shape[0], b=shape[1])
        return flat

    def region(self, at, *shape):
        flat = self.arena[:, at:at + int(np.prod(shape))]
        if len(shape) == 2:
            return flat.rearrange("p (a b) -> p a b", a=shape[0])
        if len(shape) == 3:
            return flat.rearrange("p (a b c) -> p a b c", a=shape[0], b=shape[1])
        return flat


ARENA = 24600


def regions(g, sizes):
    at, out = 0, {}
    for name, shape in sizes:
        if name == "product":
            out["arena_at"] = at
        out[name] = g.region(at, *shape)
        at += int(np.prod(shape))
    assert at <= ARENA, at
    return out



def rms_tensor(pe, n, width, group="ones", source=None):
    g = pe.g
    if pe.tiles["low"] >= 4:
        pe.wait_ge(g.sem["low_free"], pe.tiles["low"] - 3)
    tile = pe.open("low")
    for k in range(n):
        pe.wait_ge(g.sem["squares"], pe.due("squares"))
        pe.mm(tile[:, 0:width], g.const(group), g.sq[:, k, 0:width] if source is None else source, k == 0, k == n - 1,
              full="low" if k == n - 1 else None)


def rms_scalar(act, sources, width, dim):
    g, nc = act.g, act.g.nc
    for k, source in enumerate(sources):
        nc.scalar.activation(g.sq[:, k, 0:width], source, ACT.Square).then_inc(g.sem["squares"], act.adds("squares"))
    act.wait_ge(g.sem["low_full"], act.tiles["low"] + 1)
    tile = act.tile("low", peek=True)
    act.other_frees("low")
    nc.scalar.activation(g.root[:, 0:width], tile[:, 0:width], ACT.Sqrt, scale=1.0 / dim,
                                    bias=g.eps[:, 0:1]).then_inc(g.sem["root"], act.adds("root"))


def rms_vector(dve, width):
    g, nc = dve.g, dve.g.nc
    dve.tiles["low"] += 1
    if dve.foreign["low"]:
        dve.foreign["low"] = False
        dve.wait_ge(g.sem["low_free"], dve.freed["low"])
    if dve.last_sem is not None:
        dve.wait_ge(dve.last_sem, dve.last_count)
    dve.wait_ge(g.sem["root"], dve.due("root"))
    nc.vector.reciprocal(g.rinv[:, 0:width], g.root[:, 0:width]).then_inc(g.sem["low_free"], dve.frees("low"))
    dve.wait_ge(dve.last_sem, dve.last_count)



PAIRS_FF = FT // 2
DOWN0 = 2 * PAIRS_FF
FFN_CHUNKS = 3 * PAIRS_FF


def mm3(pe, out, w, x, start, stop, full=None):
    pe.mm(out, w[0], x[0], start, False)
    pe.mm(out, w[0], x[1], False, False)
    pe.mm(out, w[1], x[0], False, stop, full=full)


def split_high(act, m, it=None):
    g = act.g
    n, s = act.chunks + m, act.splits + m
    act.wait_ge(g.landed[n % SLOTS], plus(16 * (n // SLOTS + 1), it, 16))
    if s >= 2:
        act.wait_ge(g.sem["split_used"], plus(s - 1, it, SLOTS))
    g.nc.scalar.activation(g.w_split[:, 0, s % 2, :], g.ring[:, n % SLOTS, :], ACT.Copy).then_inc(g.sem["w_high"], 1)


def split_low(dve, m, it=None):
    g = dve.g
    n, s = dve.chunks + m, dve.splits + m
    dve.wait_ge(g.sem["w_high"], plus(s + 1, it, SLOTS))
    g.nc.vector.tensor_tensor(g.w_split[:, 1, s % 2, :], g.ring[:, n % SLOTS, :], g.w_split[:, 0, s % 2, :].bitcast(F32),
                              ALU.subtract).then_inc(g.sem["weights_used"], 1)


def plus(value, it, per_trip):
    return value if it is None else it * per_trip + value


def ffn_tensor(pe, width):
    g = pe.g

    def split_chunk(m, it=None):
        n, s = pe.chunks + m, pe.splits + m
        pe.wait_ge(g.sem["weights_used"], plus(n + 1, it, SLOTS))
        return [g.w_split[:, part, s % 2, :] for part in range(2)]

    def pair(p, it=None):
        for i, side in enumerate(("low", "high")):
            w = [part.rearrange("p (k n) -> p k n", k=KT) for part in split_chunk(2 * p + i, it)]
            for f in range(2):
                t = tiles[side] + 2 * p + f
                if t >= 4:
                    pe.wait_ge(g.sem[side + "_free"], plus(t - 3, it, 4))
                for k in range(KT):
                    if p == 0 and i == 0 and f == 0:
                        pe.wait_ge(g.sem["x_split"], pe.due("x_split"))
                    mm3(pe, g.banks[side][t % 4][:, 0:width], [part[:, k, f * P:(f + 1) * P] for part in w],
                        [g.x_split[:, part, k, 0:width] for part in range(2)], k == 0, k == KT - 1,
                        side if k == KT - 1 else None)
            pe.release("split_used")

    tiles = dict(pe.tiles)
    for p in range(2):
        pair(p)
    with pe.engine.Fori(0, (PAIRS_FF - 3) // 2) as it:
        for p in range(2, 4):
            pair(p, it)
    pair(PAIRS_FF - 1)
    for side in ("low", "high"):
        pe.tiles[side] += FT

    outs = []
    pe.wait_ge(g.sem["low_free"], pe.tiles["low"])
    pe.wait_ge(g.sem["high_free"], pe.tiles["high"])
    for side in ("low", "high"):
        for _ in range(4):
            outs.append(pe.open(side))

    def down(c, it=None, start=False, stop=False):
        w = [part.rearrange("p (f n) -> p f n", f=2) for part in split_chunk(DOWN0 + c, it)]
        for f in range(2):
            for j in range(KT):
                side = "low" if j < 4 else "high"
                mm3(pe, outs[j][:, 0:width], [part[:, f, j * P:(j + 1) * P] for part in w],
                    [g.a_split[:, part, c % 2, f, 0:width] for part in range(2)], start and f == 0, stop and f == 1,
                    side if stop and f == 1 else None)
        pe.release("split_used")

    for c in range(2):
        down(c, start=c == 0)
    with pe.engine.Fori(0, 2) as it:
        for c in range(2, 6):
            down(c, it)
    down(PAIRS_FF - 1, stop=True)
    pe.chunks += FFN_CHUNKS
    pe.splits += FFN_CHUNKS


def ffn_scalar(act, width):
    g, nc = act.g, act.g.nc
    act_in = g.region(0, FT, 2 * TOK)
    low, high = act.tiles["low"], act.tiles["high"]

    def gate(f, it=None):
        act.wait_ge(g.sem["low_full"], plus(low + f + 1, it, 4))
        if f >= 2:
            act.wait_ge(g.sem["high_free"], plus(high + f - 1, it, 4))
        nc.scalar.activation(g.silu[:, f % 2, 0:width], g.banks["low"][(low + f) % 4][:, 0:width],
                             ACT.Silu).then_inc(g.sem["low_free"], 1)

    def high_parts(c, it=None):
        if c in (0, 1):
            act.wait_ge(g.sem["high_free"], high + 2 * c + 2)
        at = 2 * c if it is None else it * 8 + 2 * c
        nc.scalar.activation(g.a_split[:, 0, c % 2, :, 0:width], act_in[:, bass.ds(at, 2), 0:width],
                             ACT.Copy).then_inc(g.sem["a_high"], 1)

    def pair(p, it=None, last=False):
        gate(2 * p, it)
        if last:
            high_parts(0)
        split_high(act, 2 * p + 2, it)
        gate(2 * p + 1, it)
        if last:
            high_parts(1)
        split_high(act, 2 * p + 3, it)

    for p in range(2):
        pair(p)
    with act.engine.Fori(0, (PAIRS_FF - 3) // 2) as it:
        for p in range(2, 4):
            pair(p, it)
    pair(PAIRS_FF - 1, last=True)
    act.wait_ge(g.sem["high_free"], high + FT)

    def ahead(c, it=None):
        split_high(act, DOWN0 + c + 2, it)
        high_parts(c + 2, it)

    ahead(0)
    with act.engine.Fori(0, 2) as it:
        for c in range(1, 5):
            ahead(c, it)
    act.skip("low", FT + 4)
    act.skip("high", FT + 4)


def ffn_vector(dve, width, add):
    g, nc = dve.g, dve.g.nc
    act_in = g.region(0, FT, 2 * TOK)
    low, high, inputs = dve.tiles["low"], dve.tiles["high"], dve.splits // 3

    def up(f, it=None):
        dve.wait_ge(g.sem["low_free"], plus(low + f + 1, it, 4))
        dve.wait_ge(g.sem["high_full"], plus(high + f + 1, it, 4))
        out = act_in[:, f, 0:width] if it is None else act_in[:, it * 4 + f, 0:width]
        nc.vector.tensor_tensor(out, g.silu[:, f % 2, 0:width], g.banks["high"][(high + f) % 4][:, 0:width],
                                ALU.mult).then_inc(g.sem["high_free"], 1)

    def low_parts(c, it=None):
        dve.wait_ge(g.sem["a_high"], plus(inputs + c + 1, it, 4))
        at = 2 * c if it is None else it * 8 + 2 * c
        nc.vector.tensor_tensor(g.a_split[:, 1, c % 2, :, 0:width], act_in[:, bass.ds(at, 2), 0:width],
                                g.a_split[:, 0, c % 2, :, 0:width].bitcast(F32), ALU.subtract)

    def pair(p, it=None, last=False):
        if last:
            low_parts(0)
        split_low(dve, 2 * p + 2, it)
        up(2 * p, it)
        up(2 * p + 1, it)
        if last:
            low_parts(1)
        split_low(dve, 2 * p + 3, it)

    for p in range(2):
        pair(p)
    with dve.engine.Fori(0, (PAIRS_FF - 3) // 2) as it:
        for p in range(2, 4):
            pair(p, it)
    pair(PAIRS_FF - 1, last=True)
    dve.wait_ge(g.sem["high_free"], high + FT)

    def ahead(c, it=None):
        low_parts(c + 2, it)
        split_low(dve, DOWN0 + c + 2, it)

    ahead(0)
    with dve.engine.Fori(0, 2) as it:
        for c in range(1, 5):
            ahead(c, it)
    dve.skip("low", FT)
    dve.skip("high", FT)
    for j in range(KT):
        side = "low" if j < 4 else "high"
        dve.wait_ge(g.sem[side + "_full"], dve.tiles[side] + 1)
        add(j, dve.tile(side), side)


def split_input_scalar(act, width, shift=None):
    g, nc = act.g, act.g.nc
    for k in range(KT):
        act.wait_ge(g.sem["scaled"], act.due("scaled"))
        tmp = g.silu[:, k % 2, 0:width]
        if shift is not None:
            for s in range(width // TOK):
                part = g.silu[:, k % 2, s * TOK:(s + 1) * TOK]
                nc.scalar.activation(part, part, ACT.Identity, bias=shift(k, s)).then_inc(g.sem["act_step"], act.adds("act_step"))
            act.wait_ge(act.last_sem, act.last_count)
        nc.scalar.activation(g.x_split[:, 0, k, 0:width], tmp, ACT.Copy).then_inc(g.sem["x_high"], act.adds("x_high"))


def split_input_vector(dve, width, factor):
    g, nc = dve.g, dve.g.nc
    v = nc.vector

    def low(k):
        dve.wait_ge(g.sem["x_high"], dve.due("x_high"))
        v.tensor_tensor(g.x_split[:, 1, k, 0:width], g.silu[:, k % 2, 0:width], g.x_split[:, 0, k, 0:width].bitcast(F32),
                        ALU.subtract).then_inc(g.sem["x_split"], dve.adds("x_split"))

    for k in range(KT):
        if k >= 2:
            low(k - 2)
            dve.wait_ge(dve.last_sem, dve.last_count)
        for s in range(width // TOK):
            cols = slice(s * TOK, (s + 1) * TOK)
            v.scalar_tensor_tensor(g.silu[:, k % 2, cols], g.h[:, k, cols], factor(k, s), g.rinv[:, cols],
                                   ALU.mult, ALU.mult).then_inc(
                g.sem["scaled" if s == width // TOK - 1 else "vec_step"],
                dve.adds("scaled" if s == width // TOK - 1 else "vec_step"))
    low(KT - 2)
    low(KT - 1)


def residual_add(dve, j, tile, side, factor, signal=False):
    g = dve.g
    g.nc.vector.scalar_tensor_tensor(g.h[:, j, 0:TOK], tile[:, 0:TOK], factor, g.h[:, j, 0:TOK],
                                              ALU.mult, ALU.add).then_inc(g.sem[side + "_free"], dve.frees(side))



def x_tiles(g):
    return [g.h[:, k, 0:TOK] for k in range(KT)]


def plain_norm_vector(dve, gain, n=KT, width=TOK):
    g = dve.g
    rms_vector(dve, width)
    for k in range(n):
        g.nc.vector.scalar_tensor_tensor(g.xn[:, k, 0:width], g.h[:, k, 0:width], gain[:, k:k + 1],
                                                    g.rinv[:, 0:width], ALU.mult, ALU.mult).then_inc(g.sem["normed"], dve.adds("normed"))


def ffn1_tensor(pe, l, kind):
    rms_tensor(pe, KT, TOK)
    ffn_tensor(pe, TOK)


def h_written(engine):
    if engine.freed["high"]:
        engine.wait_ge(engine.g.sem["high_free"], engine.freed["high"])


def first_splits_scalar(act):
    split_high(act, 0)
    split_high(act, 1)


def first_splits_vector(dve):
    g = dve.g
    if dve.chunks:
        dve.wait_ge(g.sem["weights_used"], dve.chunks)
    split_low(dve, 0)
    split_low(dve, 1)


def ffn1_scalar(act, l, kind):
    g = act.g
    if kind == "ffn1":
        act.wait_ge(g.sem["residual" if l else "x_in"], act.due("residual" if l else "x_in", KT if l else 16))
    else:
        h_written(act)
    first_splits_scalar(act)
    rms_scalar(act, x_tiles(g), TOK, D)
    split_input_scalar(act, TOK)
    ffn_scalar(act, TOK)


def ffn1_vector(dve, l, kind):
    g = dve.g
    first_splits_vector(dve)
    rms_vector(dve, TOK)
    gain = g.vec(f"{kind}_norm{l}")
    split_input_vector(dve, TOK, lambda k, s: gain[:, k:k + 1])
    ffn_vector(dve, TOK, lambda j, tile, side: residual_add(dve, j, tile, side, 0.5))



def mix1_buffers(g):
    r = regions(g, [
        ("latents", (5, TOK)),
        ("k_rope", (TOK,)),
        ("k_rot", (TOK,)),
        ("m_x", (2, TOK + 4)),
        ("gate_tok", (2, 16)),
        ("m_v", (2, 256)),
        ("m_o", (2, TOK)),
        ("f_in", (2, TOK)),
        ("q_nope", (HEADS, TOK)),
        ("q_rope", (2, TOK)),
        ("q_rot", (2, TOK)),
        ("k_nope", (HEADS, TOK)),
        ("v", (2, HEADS * VDIM)),
        ("rot_tmp", (TOK,)),
        ("probs", (HEADS, 2, TOK)),
        ("probs_t", (2, 2, TOK)),
        ("neg_max", (HEADS, 2)),
        ("row_sum", (HEADS, 2)),
        ("conv", (2, TOK)),
        ("conv_act", (2, TOK)),
        ("lstm_qk", (2, 512)),
        ("gate_i", (2, TOK)),
        ("gate_f", (2, TOK)),
        ("gate_t", (2, TOK)),
        ("gate_l", (2, TOK)),
        ("level", (2, TOK)),
        ("peak", (2, TOK)),
        ("neg_peak", (2, TOK)),
        ("floor", (2, TOK)),
        ("level_col", (2, 2, HEADS)),
        ("w_exp", (2, 2, 512)),
        ("weighted", (2, 2, 512)),
        ("den", (TOK,)),
        ("den2", (TOK,)),
        ("hsum", (2, TOK)),
        ("hdir", (TOK,)),
        ("fnet_ab", (2, 2, 256)),
    ])
    r["osig"] = g.xn[:, 1:3, 0:TOK]
    r["fnet_y"] = g.xn[:, 3:5, 0:TOK]
    return r


def mix1_tensor(pe, l, kind):
    g = pe.g
    b = mix1_buffers(g)
    ident, rotate = g.const("identity"), g.const("rotate")
    xn = g.xn
    rms_tensor(pe, KT, TOK)

    first = True
    def feature_tile(w, m, n=P):
        nonlocal first
        pe.wait_ge(g.sem["low_free"], pe.tiles["low"] - 3)
        tile = pe.open("low")
        for k in range(KT):
            if first:
                pe.wait_ge(g.sem["normed"], pe.due("normed"))
            pe.mm(tile[0:n, 0:TOK], w[:, k, m * P:m * P + n], xn[:, k, 0:TOK], k == 0, k == KT - 1,
                  full="low" if k == KT - 1 else None)
        first = False

    def token_tiles(w, n, separate):
        if not separate:
            pe.wait_ge(g.sem["low_free"], pe.tiles["low"] - 3)
            tile = pe.open("low")
        for t in range(2):
            if separate:
                pe.wait_ge(g.sem["low_free"], pe.tiles["low"] - 3)
                tile = pe.open("low")
            out = tile[:, 0:n] if separate else tile[:, t * n:(t + 1) * n]
            for k in range(KT):
                pe.mm(out, xn[:, k, t * P:(t + 1) * P], w[:, k, 0:n], k == 0, k == KT - 1,
                      full="low" if k == KT - 1 and (separate or t == 1) else None)

    for _ in range(4):
        pe.wait_ge(g.landed[pe.chunks % SLOTS], 16 * (pe.chunks // SLOTS + 1))
        w = pe.chunk(KT, 256)
        feature_tile(w, 0)
        feature_tile(w, 1)
        pe.release()
    pe.wait_ge(g.landed[pe.chunks % SLOTS], 16 * (pe.chunks // SLOTS + 1))
    w = pe.chunk(KT, 16)
    token_tiles(w, 16, separate=False)
    pe.release()
    pe.wait_ge(g.landed[pe.chunks % SLOTS], 16 * (pe.chunks // SLOTS + 1))
    w = pe.chunk(KT, 256)
    token_tiles(w, 256, separate=True)
    pe.release()
    for _ in range(2):
        pe.wait_ge(g.landed[pe.chunks % SLOTS], 16 * (pe.chunks // SLOTS + 1))
        w = pe.chunk(KT, 256)
        feature_tile(w, 0)
        feature_tile(w, 1)
        pe.release()

    rms_tensor(pe, 3, TOK)
    rms_tensor(pe, 2, TOK)
    for which in range(2):
        pe.wait_ge(g.sem["high_free"], pe.tiles["high"] - 3)
        tile = pe.open("high")
        for d in range(2):
            for t in range(2):
                at = which * 8 + d * 4
                out = tile[0:HEADS, d * TOK + t * P:d * TOK + (t + 1) * P]
                pe.transpose(out, b["gate_tok"][:, t, at:at + HEADS], full="high" if d == 1 and t == 1 else None)
    pe.wait_ge(g.sem["high_free"], pe.tiles["high"] - 3)
    tile = pe.open("high")
    pe.mm(tile[:, 0:TOK], rotate, b["k_rope"], full="high")

    pe.wait_ge(g.landed[pe.chunks % SLOTS], 16 * (pe.chunks // SLOTS + 1))
    w = pe.chunk(3, HEADS * NOPE)
    pe.wait_ge(g.sem["latent"], pe.due("latent", 3))
    for h in range(HEADS):
        pe.wait_ge(g.sem["low_free"], pe.tiles["low"] - 3)
        tile = pe.open("low")
        for k in range(3):
            pe.mm(tile[:, 0:TOK], w[:, k, h * P:(h + 1) * P], b["latents"][:, k, :], k == 0, k == 2,
                  full="low" if k == 2 else None)
    pe.release()
    pe.wait_ge(g.landed[pe.chunks % SLOTS], 16 * (pe.chunks // SLOTS + 1))
    w = pe.chunk(3, HEADS * ROPE)
    for p in range(2):
        pe.wait_ge(g.sem["low_free"], pe.tiles["low"] - 3)
        tile = pe.open("low")
        for k in range(3):
            pe.mm(tile[:, 0:TOK], w[:, k, p * P:(p + 1) * P], b["latents"][:, k, :], k == 0, k == 2,
                  full="low" if k == 2 else None)
    pe.release()
    pe.wait_ge(g.landed[pe.chunks % SLOTS], 16 * (pe.chunks // SLOTS + 1))
    w = pe.chunk(2, HEADS * 256)
    pe.wait_ge(g.sem["latent"], pe.due("latent", 2))
    for h in range(HEADS):
        pe.wait_ge(g.sem["low_free"], pe.tiles["low"] - 3)
        tile = pe.open("low")
        for k in range(2):
            pe.mm(tile[:, 0:TOK], w[:, k, h * 256:h * 256 + P], b["latents"][:, 3 + k, :], k == 0, k == 1,
                  full="low" if k == 1 else None)
    values = w[:, :, :].rearrange("p k (h n) -> p k h n", h=HEADS)
    for t in range(2):
        pe.wait_ge(g.sem["low_free"], pe.tiles["low"] - 3)
        tile = pe.open("low")
        for k in range(2):
            pe.mm(tile[:, :], b["latents"][:, 3 + k, t * P:(t + 1) * P], values[:, k, :, P:2 * P], k == 0, k == 1,
                  full="low" if k == 1 else None)
    pe.release()
    pe.wait_ge(g.sem["low_free"], pe.tiles["low"] - 6)
    for p in range(2):
        pe.wait_ge(g.sem["high_free"], pe.tiles["high"] - 3)
        tile = pe.open("high")
        pe.mm(tile[:, 0:TOK], rotate, b["q_rope"][:, p, :], full="high")

    pe.wait_ge(g.landed[pe.chunks % SLOTS], 16 * (pe.chunks // SLOTS + 1))
    w = pe.chunk(CHUNK)
    pe.wait_ge(g.sem["conv_act"], pe.due("conv_act", 2))
    for p in range(2):
        pe.wait_ge(g.sem["low_free"], pe.tiles["low"] - 3)
        tile = pe.open("low")
        pe.mm(tile[:, 0:TOK], w[:, p * P:(p + 1) * P], b["conv_act"][:, p, :])
        pe.mm(tile[:, TOK:2 * TOK], w[:, 256 + p * P:256 + (p + 1) * P], b["conv_act"][:, p, :], full="low")
    channel = w[:, 768:1024]
    for t in range(2):
        for p in range(2):
            pe.wait_ge(g.sem["low_free"], pe.tiles["low"] - 3)
            tile = pe.open("low")
            pe.mm(tile[:, 0:256], b["f_in"][:, p, t * P:(t + 1) * P], channel, full="low")
    pe.wait_ge(g.sem["low_free"], pe.tiles["low"])
    for p in range(2):
        pe.wait_ge(g.sem["low_free"], pe.tiles["low"] - 3)
        tile = pe.open("low")
        n = 0
        for t in range(2):
            for part in range(2):
                place = w[:, 1024 + part * 512 + t * TOK:1024 + part * 512 + (t + 1) * TOK]
                pe.mm(tile[:, 0:TOK], b["fnet_ab"][:, t, p, part * P:(part + 1) * P], place, n == 0, n == 3,
                      full="low" if n == 3 else None)
                n += 1

    pe.wait_ge(g.sem["rotated"], pe.due("rotated", 3))
    for h in range(HEADS):
        pe.wait_ge(g.sem["low_free"], pe.tiles["low"] - 3)
        tile = pe.open("low")
        base = 64 * (h % 2)
        for q in range(2):
            out = tile[:, q * TOK:(q + 1) * TOK]
            pe.mm(out, b["q_nope"][:, h, q * P:(q + 1) * P], b["k_nope"][:, h, :], True, False)
            pe.mm(out, b["q_rot"][base:base + 64, h // 2, q * P:(q + 1) * P], b["k_rot"][base:base + 64, :],
                  False, True, full="low" if q == 1 else None)
    pe.wait_ge(g.sem["low_free"], pe.tiles["low"] - 4)
    for p in range(2):
        pe.wait_ge(g.sem["high_free"], pe.tiles["high"] - 3)
        tile = pe.open("high")
        pe.mm(tile[:, 0:TOK], w[:, 512 + p * P:512 + (p + 1) * P], b["fnet_y"][:, p, :], full="high")
    pe.release()
    pe.wait_ge(g.sem["gate_rows"], pe.due("gate_rows"))
    pe.wait_ge(g.sem["high_free"], pe.tiles["high"] - 3)
    tile = pe.open("high")
    for d in range(2):
        for t in range(2):
            at = (d * 2 + t) * HEADS
            pe.transpose(tile[:, at:at + HEADS], b["level"][0:HEADS, d, t * P:(t + 1) * P],
                         full="high" if d == 1 and t == 1 else None)
    for h in range(HEADS):
        pe.wait_ge(g.sem["high_free"], pe.tiles["high"] - 3)
        tile = pe.open("high")
        pe.wait_ge(g.sem["probs_scaled"], pe.due("probs_scaled", 2))
        for t in range(2):
            for q in range(2):
                pe.transpose(tile[:, t * TOK + q * P:t * TOK + (q + 1) * P], b["probs"][:, h, q, t * P:(t + 1) * P],
                             full="high" if t == 1 and q == 1 else None)
        pe.wait_ge(g.sem["high_free"], pe.tiles["high"])
        pe.wait_ge(g.sem["low_free"], pe.tiles["low"] - 3)
        tile = pe.open("low")
        for t in range(2):
            pe.mm(tile[:, 0:TOK], b["v"][:, t, h * P:(h + 1) * P], b["probs_t"][:, h % 2, t, :], t == 0, t == 1,
                  full="low" if t == 1 else None)

    for p in range(2):
        for h in (2 * p, 2 * p + 1):
            base = LH * (h % 2)
            pe.wait_ge(g.sem["high_free"], pe.tiles["high"] - 3)
            tile = pe.open("high")
            pe.mm(tile[:, :], g.const("select")[0:HEADS, h, :], b["neg_peak"][0:HEADS, :, :], full="high")
            pe.wait_ge(g.sem["high_free"], pe.tiles["high"] - 3)
            tile = pe.open("high")
            for t in range(2):
                pe.mm(tile[:, t * TOK:(t + 1) * TOK], b["lstm_qk"][base:base + LH, p, TOK + t * P:TOK + (t + 1) * P],
                      b["lstm_qk"][base:base + LH, p, 0:TOK], full="high" if t == 1 else None)
        for d in range(2):
            if d == 0:
                pe.wait_ge(g.sem["weighted"], pe.due("weighted", 2))
                pe.wait_ge(g.sem["high_free"], pe.tiles["high"])
            pe.wait_ge(g.sem["high_free"], pe.tiles["high"] - 3)
            tile = pe.open("high")
            pe.mm(tile[:, 0:TOK], g.const("select_pair")[0:HEADS, p, :], b["floor"][0:HEADS, d, :], full="high")
            pe.wait_ge(g.sem["high_free"], pe.tiles["high"] - 3)
            tile = pe.open("high")
            for h in (2 * p, 2 * p + 1):
                base = LH * (h % 2)
                for part, lhs in enumerate((None, g.const("ones")[:, 0:LH])):
                    for t in range(2):
                        lhsT = b["m_v"][:, t, h * LH:(h + 1) * LH] if lhs is None else lhs
                        pe.mm(tile[base:base + LH, part * TOK:(part + 1) * TOK], lhsT,
                              b["weighted"][:, d, h % 2, t * TOK:(t + 1) * TOK], t == 0, t == 1,
                              full="high" if h % 2 and part and t else None)
        pe.wait_ge(g.sem["low_free"], pe.tiles["low"] - 3)
        tile = pe.open("low")
        pe.wait_ge(g.sem["squares"], pe.due("squares"))
        pe.mm(tile[:, 0:TOK], g.const("head_ones"), g.xn[:, 0, 0:TOK], full="low")

    pe.wait_ge(g.sem["mix_done"], pe.due("mix_done", 2))
    pe.wait_ge(g.sem["low_free"], pe.tiles["low"])
    out_projection(pe, TOK)


def out_projection(pe, width):
    g = pe.g
    for _ in range(KT // 2):
        pe.wait_ge(g.landed[pe.chunks % SLOTS], 16 * (pe.chunks // SLOTS + 1))
        w = pe.chunk(KT, 256)
        for m in range(2):
            pe.wait_ge(g.sem["high_free"], pe.tiles["high"] - 3)
            tile = pe.open("high")
            for k in range(KT):
                pe.mm(tile[:, 0:width], w[:, k, m * P:(m + 1) * P], g.sq[:, k, 0:width], k == 0, k == KT - 1,
                      full="high" if k == KT - 1 else None)
        pe.release()


def mix1_scalar(act, l, kind):
    g, nc = act.g, act.g.nc
    b = mix1_buffers(g)
    A = nc.scalar.activation

    h_written(act)
    rms_scalar(act, x_tiles(g), TOK, D)
    for k in range(5):
        act.wait_ge(g.sem["low_full"], act.tiles["low"] + 1)
        A(b["latents"][:, k, :], act.tile("low")[:, 0:TOK], ACT.Copy).then_inc(g.sem["low_free"], act.frees("low"))
    act.wait_ge(g.sem["low_full"], act.tiles["low"] + 1)
    A(b["k_rope"], act.tile("low")[:, 0:TOK], ACT.Copy).then_inc(g.sem["low_free"], act.frees("low"))
    for p in range(2):
        act.wait_ge(g.sem["low_full"], act.tiles["low"] + 1)
        A(b["m_x"][:, p, 2:2 + TOK], act.tile("low")[:, 0:TOK], ACT.Copy).then_inc(g.sem["low_free"], act.frees("low"))
    act.wait_ge(g.sem["low_full"], act.tiles["low"] + 1)
    A(b["gate_tok"], act.tile("low")[:, 0:32].rearrange("p (t n) -> p t n", t=2), ACT.Copy).then_inc(g.sem["low_free"], act.frees("low"))
    for t in range(2):
        act.wait_ge(g.sem["low_full"], act.tiles["low"] + 1)
        A(b["m_v"][:, t, :], act.tile("low")[:, 0:256], ACT.Copy).then_inc(g.sem["low_free"], act.frees("low"))
    for p in range(2):
        act.wait_ge(g.sem["low_full"], act.tiles["low"] + 1)
        A(b["m_o"][:, p, :], act.tile("low")[:, 0:TOK], ACT.Copy).then_inc(g.sem["low_free"], act.frees("low"))
    for p in range(2):
        act.wait_ge(g.sem["low_full"], act.tiles["low"] + 1)
        A(b["f_in"][:, p, :], act.tile("low")[:, 0:TOK], ACT.Copy).then_inc(g.sem["low_free"], act.frees("low"))
    act.wait_ge(act.last_sem, act.last_count)
    rms_scalar(act, [b["latents"][:, k, :] for k in range(3)], TOK, Q_LORA)
    act.wait_ge(g.sem["low_free"], act.freed["low"])
    rms_scalar(act, [b["latents"][:, k, :] for k in range(3, 5)], TOK, KV_LORA)
    for h in range(HEADS):
        act.wait_ge(g.sem["low_full"], act.tiles["low"] + 1)
        A(b["q_nope"][:, h, :], act.tile("low")[:, 0:TOK], ACT.Copy).then_inc(g.sem["low_free"], act.frees("low"))
    for p in range(2):
        act.wait_ge(g.sem["low_full"], act.tiles["low"] + 1)
        A(b["q_rope"][:, p, :], act.tile("low")[:, 0:TOK], ACT.Copy).then_inc(g.sem["low_free"], act.frees("low"))
    for h in range(HEADS):
        act.wait_ge(g.sem["low_full"], act.tiles["low"] + 1)
        A(b["k_nope"][:, h, :], act.tile("low")[:, 0:TOK], ACT.Copy).then_inc(g.sem["low_free"], act.frees("low"))
    for t in range(2):
        act.wait_ge(g.sem["low_full"], act.tiles["low"] + 1)
        A(b["v"][:, t, :], act.tile("low")[:, :], ACT.Copy).then_inc(g.sem["low_free"], act.frees("low"))
    for p in range(2):
        act.wait_ge(g.sem["conv_out"], act.due("conv_out"))
        A(b["conv_act"][:, p, :], b["conv"][:, p, :], ACT.Silu, bias=g.vec(f"conv_b{l}")[:, p:p + 1]).then_inc(g.sem["conv_act"], act.adds("conv_act"))
    for p in range(2):
        act.wait_ge(g.sem["low_full"], act.tiles["low"] + 1)
        tile = act.tile("low")
        A(b["lstm_qk"][:, p, 0:TOK], tile[:, 0:TOK], ACT.Copy, scale=LH ** -0.5).then_inc(g.sem["act_step"], act.adds("act_step"))
        A(b["lstm_qk"][:, p, TOK:2 * TOK], tile[:, TOK:2 * TOK], ACT.Copy).then_inc(g.sem["low_free"], act.frees("low"))
    for t in range(2):
        for p in range(2):
            act.wait_ge(g.sem["low_full"], act.tiles["low"] + 1)
            A(b["fnet_ab"][:, t, p, :], act.tile("low")[:, 0:256], ACT.Copy).then_inc(g.sem["low_free"], act.frees("low"))
    for p in range(2):
        act.wait_ge(g.sem["low_full"], act.tiles["low"] + 1)
        A(b["fnet_y"][:, p, :], act.tile("low")[:, 0:TOK], ACT.Copy).then_inc(g.sem["low_free"], act.frees("low"))
    for p in range(2):
        A(b["osig"][:, p, :], b["m_o"][:, p, :], ACT.Sigmoid).then_inc(g.sem["act_step"], act.adds("act_step"))
    act.wait_ge(g.sem["gate_abs"], act.due("gate_abs"))
    A(b["gate_t"][0:HEADS], b["gate_t"][0:HEADS], ACT.Exp, scale=-1.0).then_inc(g.sem["act_step"], act.adds("act_step"))
    act.wait_ge(act.last_sem, act.last_count)
    A(b["gate_l"][0:HEADS], b["gate_t"][0:HEADS], ACT.Ln, bias=1.0).then_inc(g.sem["gate_ln"], act.adds("gate_ln"))
    for h in range(HEADS):
        act.wait_ge(g.sem["low_full"], act.tiles["low"] + 1)
        tile = act.tile("low")
        act.wait_ge(g.sem["neg_max"], act.due("neg_max"))
        for q in range(2):
            ins = A(b["probs"][:, h, q, :], tile[:, q * TOK:(q + 1) * TOK], ACT.Exp, scale=MLA_SCALE,
                    bias=b["neg_max"][:, h, q:q + 1], accum_out=b["row_sum"][:, h, q:q + 1])
            if q == 0:
                ins.then_inc(g.sem["act_step"], act.adds("act_step"))
            else:
                ins.then_inc(g.sem["low_free"], act.frees("low"))
    act.wait_ge(g.sem["gate_exp"], act.due("gate_exp"))
    A(b["floor"][0:HEADS], b["floor"][0:HEADS], ACT.Exp, scale=-1.0).then_inc(g.sem["floor_done"], act.adds("floor_done"))
    for h in range(HEADS):
        act.wait_ge(g.sem["low_full"], act.tiles["low"] + 1)
        A(g.sq[:, h, 0:TOK], act.tile("low")[:, 0:TOK], ACT.Copy).then_inc(g.sem["low_free"], act.frees("low"))
    act.skip("high", MIX1_HIGH - 16 - KT)
    for p in range(2):
        for h in (2 * p, 2 * p + 1):
            act.skip("high")
            for d in range(2):
                if d == 0:
                    act.wait_ge(g.sem["decay_in"], act.due("decay_in"))
                else:
                    act.wait_ge(g.sem["high_free"], act.freed["high"])
                for t in range(2):
                    ins = A(b["w_exp"][:, d, h % 2, t * TOK:(t + 1) * TOK], b["w_exp"][:, d, h % 2, t * TOK:(t + 1) * TOK],
                            ACT.Exp, bias=b["level_col"][:, d, t, h:h + 1])
                    if t:
                        ins.then_inc(g.sem["decay"], act.adds("decay"))
                    else:
                        ins.then_inc(g.sem["act_step"], act.adds("act_step"))
            act.skip("high")
        act.skip("high", 4)
        act.wait_ge(g.sem["out_done"], act.due("out_done"))
        A(g.xn[:, 0, 0:TOK], b["hsum"][:, p, :], ACT.Square).then_inc(g.sem["squares"], act.adds("squares"))
        act.wait_ge(g.sem["low_full"], act.tiles["low"] + 1)
        tile = act.tile("low", peek=True)
        act.other_frees("low")
        A(g.root[:, 0:TOK], tile[:, 0:TOK], ACT.Sqrt, scale=1.0 / LH, bias=g.eps[:, 0:1]).then_inc(g.sem["root"], act.adds("root"))
    act.skip("high", KT)


MIX1_HIGH = 2 + 1 + 2 + 2 + 1 + HEADS + 2 * (4 + 4) + KT


def rotate_vector(dve, out, raw, tile, tmp, cos, sin, signal="rotated"):
    g, nc = dve.g, dve.g.nc
    nc.vector.tensor_tensor(out, raw, cos, ALU.mult).then_inc(g.sem["vec_step"], dve.adds("vec_step"))
    nc.vector.tensor_tensor(tmp, tile, sin, ALU.mult).then_inc(g.sem["high_free"], dve.frees("high"))
    dve.wait_ge(dve.last_sem, dve.last_count)
    nc.vector.tensor_tensor(out, out, tmp, ALU.add).then_inc(g.sem[signal], dve.adds(signal))
    dve.wait_ge(dve.last_sem, dve.last_count)


def mix1_vector(dve, l, kind):
    g, nc = dve.g, dve.g.nc
    v = nc.vector
    b = mix1_buffers(g)
    H = HEADS
    plain_norm_vector(dve, g.vec(f"mix_norm{l}"))
    v.memset(b["m_x"][:, :, 0:2], 0.0).then_inc(g.sem["vec_step"], dve.adds("vec_step"))
    v.memset(b["m_x"][:, :, TOK + 2:TOK + 4], 0.0).then_inc(g.sem["vec_step"], dve.adds("vec_step"))
    dve.skip("low", 15)
    for n, at, gain in ((3, 0, "q_norm"), (2, 3, "kv_norm")):
        rms_vector(dve, TOK)
        for k in range(n):
            tile = b["latents"][:, at + k, :]
            v.scalar_tensor_tensor(tile, tile, g.vec(f"{gain}{l}")[:, k:k + 1], g.rinv[:, 0:TOK],
                                              ALU.mult, ALU.mult).then_inc(g.sem["latent"], dve.adds("latent"))
    for row, bias in (("gate_i", "i_bias"), ("gate_f", "f_bias")):
        dve.wait_ge(g.sem["high_full"], dve.tiles["high"] + 1)
        tile = dve.tile("high")
        for d in range(2):
            ins = v.tensor_scalar(b[row][0:H, d, :], tile[0:H, d * TOK:(d + 1) * TOK],
                                  g.vec(f"{bias}{l}")[0:H, d:d + 1], None, ALU.add)
            if d:
                ins.then_inc(g.sem["high_free"], dve.frees("high"))
            else:
                ins.then_inc(g.sem["vec_step"], dve.adds("vec_step"))
    dve.wait_ge(dve.last_sem, dve.last_count)
    v.scalar_tensor_tensor(b["gate_t"][0:H], b["gate_f"][0:H], -1.0, b["gate_f"][0:H], ALU.mult, ALU.max).then_inc(g.sem["gate_abs"], dve.adds("gate_abs"))
    dve.wait_ge(g.sem["high_full"], dve.tiles["high"] + 1)
    tile = dve.tile("high")
    rotate_vector(dve, b["k_rot"], b["k_rope"], tile[:, 0:TOK], b["rot_tmp"], g.rope[:, 0, :], g.rope[:, 1, :])
    taps = g.vec(f"conv_w{l}")
    for p in range(2):
        x, out = b["m_x"][:, p, :], b["conv"][:, p, :]
        v.tensor_scalar(out, x[:, 0:TOK], taps[:, p * 5:p * 5 + 1], None, ALU.mult).then_inc(g.sem["vec_step"], dve.adds("vec_step"))
        for k in range(1, 5):
            dve.wait_ge(dve.last_sem, dve.last_count)
            ins = v.scalar_tensor_tensor(out, x[:, k:k + TOK], taps[:, p * 5 + k:p * 5 + k + 1], out, ALU.mult, ALU.add)
            if k < 4:
                ins.then_inc(g.sem["vec_step"], dve.adds("vec_step"))
            else:
                ins.then_inc(g.sem["conv_out"], dve.adds("conv_out"))
    dve.skip("low", 4 + 2 + 4 + 2)
    for p in range(2):
        dve.wait_ge(g.sem["high_full"], dve.tiles["high"] + 1)
        tile = dve.tile("high")
        rotate_vector(dve, b["q_rot"][:, p, :], b["q_rope"][:, p, :], tile[:, 0:TOK], b["rot_tmp"],
                      g.rope[:, 0, :], g.rope[:, 1, :])
    dve.skip("low", 2 + 4 + 2)
    dve.wait_ge(g.sem["gate_ln"], dve.due("gate_ln"))
    v.scalar_tensor_tensor(b["gate_f"][0:H], b["gate_f"][0:H], 0.0, b["gate_l"][0:H], ALU.min, ALU.subtract).then_inc(g.sem["vec_step"], dve.adds("vec_step"))
    v.memset(b["level"][0:H], 1.0).then_inc(g.sem["vec_step"], dve.adds("vec_step"))
    dve.wait_ge(dve.last_sem, dve.last_count)
    cum = b["gate_t"]
    v.tensor_tensor_scan(cum[0:H, 0, :], b["level"][0:H, 0, :], b["gate_f"][0:H, 0, :], 0.0, ALU.mult, ALU.add).then_inc(g.sem["vec_step"], dve.adds("vec_step"))
    v.tensor_tensor_scan(cum[0:H, 1, ::-1], b["level"][0:H, 1, :], b["gate_f"][0:H, 1, ::-1], 0.0,
                                  ALU.mult, ALU.add).then_inc(g.sem["vec_step"], dve.adds("vec_step"))
    dve.wait_ge(dve.last_sem, dve.last_count)
    v.tensor_tensor(b["level"][0:H], b["gate_i"][0:H], cum[0:H], ALU.subtract).then_inc(g.sem["gate_rows"], dve.adds("gate_rows"))
    dve.wait_ge(dve.last_sem, dve.last_count)
    v.tensor_tensor_scan(b["peak"][0:H, 0, :], b["level"][0:H, 0, :], b["level"][0:H, 0, :], 0.0,
                                  ALU.max, ALU.max).then_inc(g.sem["vec_step"], dve.adds("vec_step"))
    v.tensor_tensor_scan(b["peak"][0:H, 1, ::-1], b["level"][0:H, 1, ::-1], b["level"][0:H, 1, ::-1], 0.0,
                                  ALU.max, ALU.max).then_inc(g.sem["vec_step"], dve.adds("vec_step"))
    dve.wait_ge(dve.last_sem, dve.last_count)
    v.tensor_scalar(b["neg_peak"][0:H], b["peak"][0:H], -1.0, None, ALU.mult).then_inc(g.sem["vec_step"], dve.adds("vec_step"))
    v.tensor_tensor(b["floor"][0:H], b["peak"][0:H], cum[0:H], ALU.add).then_inc(g.sem["gate_exp"], dve.adds("gate_exp"))
    for h in range(H):
        dve.wait_ge(g.sem["low_full"], dve.tiles["low"] + 1)
        tile = dve.tile("low", peek=True)
        v.reduce_max(b["neg_max"][:, h, :], tile[:, :].rearrange("p (q k) -> p q k", q=2), AX).then_inc(g.sem["vec_step"], dve.adds("vec_step"))
        dve.wait_ge(dve.last_sem, dve.last_count)
        v.tensor_scalar(b["neg_max"][:, h, :], b["neg_max"][:, h, :], -MLA_SCALE, None, ALU.mult).then_inc(g.sem["neg_max"], dve.adds("neg_max"))
        dve.other_frees("low")
    for p in range(2):
        dve.wait_ge(g.sem["high_full"], dve.tiles["high"] + 1)
        tile = dve.tile("high")
        v.tensor_scalar(g.sq[:, 6 + p, 0:TOK], tile[:, 0:TOK], g.vec(f"fnet_b{l}")[:, p:p + 1], None, ALU.add).then_inc(g.sem["high_free"], dve.frees("high"))
    dve.wait_ge(g.sem["high_full"], dve.tiles["high"] + 1)
    tile = dve.tile("high")
    v.tensor_copy(b["level_col"].rearrange("p d t h -> p (d t h)"), tile[:, 0:4 * H]).then_inc(g.sem["high_free"], dve.frees("high"))
    first_low = dve.tiles["low"] - H
    for h in range(H):
        dve.wait_ge(g.sem["low_free"], first_low + h + 1)
        v.reciprocal(b["row_sum"][:, h, :], b["row_sum"][:, h, :]).then_inc(g.sem["vec_step"], dve.adds("vec_step"))
        dve.wait_ge(dve.last_sem, dve.last_count)
        for q in range(2):
            v.tensor_scalar(b["probs"][:, h, q, :], b["probs"][:, h, q, :], b["row_sum"][:, h, q:q + 1],
                                       None, ALU.mult).then_inc(g.sem["probs_scaled"], dve.adds("probs_scaled"))
    for h in range(H):
        dve.wait_ge(g.sem["high_full"], dve.tiles["high"] + 1)
        tile = dve.tile("high")
        v.tensor_copy(b["probs_t"][:, h % 2, :, :].rearrange("p t q -> p (t q)"), tile[:, :]).then_inc(g.sem["high_free"], dve.frees("high"))
    dve.skip("low", H)
    mask = g.const("lstm_mask")
    dve.wait_ge(g.sem["floor_done"], dve.due("floor_done"))
    for p in range(2):
        for h in (2 * p, 2 * p + 1):
            dve.wait_ge(g.sem["high_full"], dve.tiles["high"] + 1)
            tile = dve.tile("high")
            for d in range(2):
                for t in range(2):
                    ins = v.tensor_tensor(b["w_exp"][:, d, h % 2, t * TOK:(t + 1) * TOK], tile[:, d * TOK:(d + 1) * TOK],
                                          mask[:, d, t, :], ALU.add)
                    if t == 0:
                        ins.then_inc(g.sem["vec_step"], dve.adds("vec_step"))
                    elif d == 0:
                        ins.then_inc(g.sem["decay_in"], dve.adds("decay_in"))
                    else:
                        ins.then_inc(g.sem["high_free"], dve.frees("high"))
            dve.wait_ge(g.sem["high_full"], dve.tiles["high"] + 1)
            tile = dve.tile("high")
            for d in range(2):
                dve.wait_ge(g.sem["decay"], dve.due("decay"))
                ins = v.tensor_tensor(b["weighted"][:, d, h % 2, :], tile[:, :], b["w_exp"][:, d, h % 2, :], ALU.mult)
                if d == 0:
                    ins.then_inc(g.sem["weighted"], dve.adds("weighted"))
                else:
                    ins.then_inc(g.sem["high_free"], dve.frees("high"))
        for d in range(2):
            dve.wait_ge(g.sem["high_full"], dve.tiles["high"] + 1)
            floor = dve.tile("high")
            dve.wait_ge(g.sem["high_full"], dve.tiles["high"] + 1)
            num = dve.tile("high")
            v.tensor_scalar(b["den"], num[:, TOK:2 * TOK], -1.0, None, ALU.mult).then_inc(g.sem["vec_step"], dve.adds("vec_step"))
            dve.wait_ge(dve.last_sem, dve.last_count)
            v.tensor_tensor(b["den"], b["den"], num[:, TOK:2 * TOK], ALU.max).then_inc(g.sem["vec_step"], dve.adds("vec_step"))
            dve.wait_ge(dve.last_sem, dve.last_count)
            v.tensor_tensor(b["den2"], b["den"], floor[:, 0:TOK], ALU.max).then_inc(g.sem["high_free"], dve.frees("high"))
            dve.wait_ge(dve.last_sem, dve.last_count)
            v.reciprocal(b["den2"], b["den2"]).then_inc(g.sem["vec_step"], dve.adds("vec_step"))
            dve.wait_ge(dve.last_sem, dve.last_count)
            out = b["hsum"][:, p, :] if d == 0 else b["hdir"]
            v.tensor_tensor(out, num[:, 0:TOK], b["den2"], ALU.mult).then_inc(g.sem["high_free"], dve.frees("high"))
        dve.wait_ge(dve.last_sem, dve.last_count)
        v.tensor_tensor(b["hsum"][:, p, :], b["hsum"][:, p, :], b["hdir"], ALU.add).then_inc(g.sem["out_done"], dve.adds("out_done"))
        dve.wait_ge(dve.last_sem, dve.last_count)
        rms_vector(dve, TOK)
        out = g.sq[:, 4 + p, 0:TOK]
        v.scalar_tensor_tensor(out, b["hsum"][:, p, :], g.vec(f"head_norm{l}")[:, p:p + 1], g.rinv[:, 0:TOK],
                                        ALU.mult, ALU.mult).then_inc(g.sem["vec_step"], dve.adds("vec_step"))
        dve.wait_ge(dve.last_sem, dve.last_count)
        v.scalar_tensor_tensor(out, b["conv_act"][:, p, :], g.vec(f"skip{l}")[:, p:p + 1], out,
                                        ALU.mult, ALU.add).then_inc(g.sem["vec_step"], dve.adds("vec_step"))
        dve.wait_ge(dve.last_sem, dve.last_count)
        v.tensor_tensor(out, out, b["osig"][:, p, :], ALU.mult).then_inc(g.sem["mix_done"], dve.adds("mix_done"))
    for j in range(KT):
        dve.wait_ge(g.sem["high_full"], dve.tiles["high"] + 1)
        tile = dve.tile("high")
        v.tensor_tensor(g.h[:, j, 0:TOK], tile[:, 0:TOK], g.h[:, j, 0:TOK], ALU.add).then_inc(g.sem["high_free"], dve.frees("high"))



def ple_buffers(g):
    return regions(g, [("e", (KT, TOK)), ("gate", (KT, TOK)), ("rinv_e", (TOK,))])


def ple_tensor(pe, l, kind):
    g = pe.g
    b = ple_buffers(g)
    pe.wait_ge(g.landed[pe.chunks % SLOTS], 16 * (pe.chunks // SLOTS + 1))
    embedding = pe.chunk(2, TOK)
    pe.wait_ge(g.landed[pe.chunks % SLOTS], 16 * (pe.chunks // SLOTS + 1))
    w = pe.chunk(2, D)
    for j in range(KT):
        pe.wait_ge(g.sem["low_free"], pe.tiles["low"] - 3)
        tile = pe.open("low")
        for k in range(2):
            pe.mm(tile[:, 0:TOK], w[:, k, j * P:(j + 1) * P], embedding[:, k, :], k == 0, k == 1,
                  full="low" if k == 1 else None)
    pe.release()
    pe.release()
    rms_tensor(pe, KT, TOK)
    rms_tensor(pe, KT, TOK)
    first = True
    for _ in range(KT // 2):
        pe.wait_ge(g.landed[pe.chunks % SLOTS], 16 * (pe.chunks // SLOTS + 1))
        w = pe.chunk(KT, 256)
        for m in range(2):
            pe.wait_ge(g.sem["low_free"], pe.tiles["low"] - 3)
            tile = pe.open("low")
            for k in range(KT):
                if first:
                    pe.wait_ge(g.sem["normed"], pe.due("normed"))
                pe.mm(tile[:, 0:TOK], w[:, k, m * P:(m + 1) * P], g.xn[:, k, 0:TOK], k == 0, k == KT - 1,
                      full="low" if k == KT - 1 else None)
            first = False
        pe.release()


def ple_scalar(act, l, kind):
    g, nc = act.g, act.g.nc
    b = ple_buffers(g)
    for j in range(KT):
        act.wait_ge(g.sem["low_full"], act.tiles["low"] + 1)
        tile = act.tile("low")
        nc.scalar.activation(b["e"][:, j, :], tile[:, 0:TOK], ACT.Copy).then_inc(g.sem["low_free"], act.frees("low"))
    act.wait_ge(act.last_sem, act.last_count)
    rms_scalar(act, [b["e"][:, k, :] for k in range(KT)], TOK, D)
    h_written(act)
    act.wait_ge(g.sem["low_free"], act.freed["low"])
    rms_scalar(act, x_tiles(g), TOK, D)
    for j in range(KT):
        act.wait_ge(g.sem["low_full"], act.tiles["low"] + 1)
        tile = act.tile("low")
        nc.scalar.activation(b["gate"][:, j, :], tile[:, 0:TOK], ACT.Sigmoid).then_inc(g.sem["low_free"], act.frees("low"))


def ple_vector(dve, l, kind):
    g, nc = dve.g, dve.g.nc
    b = ple_buffers(g)
    dve.skip("low", KT)
    rms_vector(dve, TOK)
    gain = g.vec(f"ple_post_norm{l}")
    for k in range(KT):
        nc.vector.scalar_tensor_tensor(b["e"][:, k, :], b["e"][:, k, :], gain[:, k:k + 1], g.rinv[:, 0:TOK],
                                                ALU.mult, ALU.mult).then_inc(g.sem["vec_step"], dve.adds("vec_step"))
    dve.wait_ge(dve.last_sem, dve.last_count)
    plain_norm_vector(dve, g.vec(f"ple_gate_norm{l}"))
    dve.wait_ge(dve.last_sem, dve.last_count)
    for j in range(KT):
        dve.skip("low")
        dve.wait_ge(g.sem["low_free"], dve.freed["low"])
        nc.vector.tensor_tensor(b["gate"][:, j, :], b["gate"][:, j, :], b["e"][:, j, :], ALU.mult).then_inc(g.sem["vec_step"], dve.adds("vec_step"))
        dve.wait_ge(dve.last_sem, dve.last_count)
        nc.vector.tensor_tensor(g.h[:, j, 0:TOK], g.h[:, j, 0:TOK], b["gate"][:, j, :], ALU.add).then_inc(g.sem["residual"], dve.adds("residual"))



def final_tensor(pe, l, kind):
    rms_tensor(pe, KT, TOK)


def final_scalar(act, l, kind):
    g = act.g
    act.wait_ge(g.sem["residual"], act.due("residual", KT))
    rms_scalar(act, x_tiles(act.g), TOK, D)
    act.wait_ge(g.sem["final_normed"], act.due("final_normed"))


def final_vector(dve, l, kind):
    g, nc = dve.g, dve.g.nc
    rms_vector(dve, TOK)
    gain = g.vec("final_norm")
    for k in range(KT):
        ins = nc.vector.scalar_tensor_tensor(g.h[:, k, 0:TOK], g.h[:, k, 0:TOK], gain[:, k:k + 1],
                                             g.rinv[:, 0:TOK], ALU.mult, ALU.mult)
        if k == KT - 1:
            ins.then_inc(g.sem["final_normed"], dve.adds("final_normed"))
        else:
            ins.then_inc(g.sem["vec_step"], dve.adds("vec_step"))
    dve.wait_ge(dve.last_sem, dve.last_count)



STREAMS = 2
BOTH = STREAMS * TOK


ADA_CHUNKS = 9 * D // 256


def ada_rows(g):
    return g.region(0, 9 * D)[0:STREAMS]


def ada_tensor(pe, l, kind):
    g = pe.g
    if "mod_in" not in pe.seen:
        pe.wait_ge(g.sem["mod_in"], pe.due("mod_in"))

    def chunk(c, it=None):
        n, t = pe.chunks + c, pe.tiles["low"] + c
        pe.wait_ge(g.landed[n % SLOTS], plus(16 * (n // SLOTS + 1), it, 16))
        if c >= 4:
            pe.wait_ge(g.sem["low_free"], plus(t - 3, it, SLOTS))
        w = g.slot(n, KT, 256)
        for k in range(KT):
            pe.mm(g.banks["low"][t % 4][0:STREAMS, 0:256], g.cond[:, k, :], w[:, k, :], k == 0, k == KT - 1,
                  full="low" if k == KT - 1 else None)
        pe.release()

    if pe.tiles["low"]:
        pe.wait_ge(g.sem["low_free"], pe.tiles["low"])
    for c in range(SLOTS):
        chunk(c)
    with pe.engine.Fori(0, ADA_CHUNKS // SLOTS - 1) as it:
        for c in range(SLOTS):
            chunk(SLOTS + c, it)
    pe.chunks += ADA_CHUNKS
    pe.tiles["low"] += ADA_CHUNKS
    pe.wait_ge(g.sem["low_free"], pe.tiles["low"])
    pe.wait_ge(g.sem["high_free"], pe.tiles["high"] - 3)
    tile = pe.open("high")
    for n in range(9 * KT):
        pe.transpose(tile[:, n * STREAMS:(n + 1) * STREAMS], ada_rows(g)[:, n * P:(n + 1) * P],
                     full="high" if n == 9 * KT - 1 else None)


def ada_scalar(act, l, kind):
    g, nc = act.g, act.g.nc
    if "mod_in" not in act.made:
        nc.scalar.activation(g.cond[:, :, :], g.vec("cond").rearrange("p (k s) -> p k s", s=STREAMS),
                             ACT.Silu).then_inc(g.sem["mod_in"], act.adds("mod_in"))
    low = act.tiles["low"]
    with act.engine.Fori(0, ADA_CHUNKS // SLOTS) as it:
        for c in range(SLOTS):
            act.wait_ge(g.sem["low_full"], plus(low + c + 1, it, SLOTS))
            nc.scalar.activation(ada_rows(g)[:, bass.ds(it * (SLOTS * 256) + c * 256, 256)],
                                 g.banks["low"][(low + c) % 4][0:STREAMS, 0:256], ACT.Copy).then_inc(g.sem["low_free"], 1)
    act.skip("low", ADA_CHUNKS)
    act.skip("high")


def ada_vector(dve, l, kind):
    g, nc = dve.g, dve.g.nc
    v = nc.vector
    dve.skip("low", ADA_CHUNKS)
    dve.wait_ge(dve.last_sem, dve.last_count)
    dve.wait_ge(g.sem["high_full"], dve.tiles["high"] + 1)
    tile = dve.tile("high")
    flat = g.mod[:, :, :, :].rearrange("p n k s -> p (n k) s")
    source = tile[:, 0:9 * KT * STREAMS].rearrange("p (n s) -> p n s", s=STREAMS)
    v.tensor_tensor(flat[:, :, 0], source[:, :, 0], g.vec(f"ada_b{l}"), ALU.add).then_inc(g.sem["vec_step"], dve.adds("vec_step"))
    v.tensor_tensor(flat[:, :, 1], source[:, :, 1], g.vec(f"ada_b{l}"), ALU.add).then_inc(g.sem["high_free"], dve.frees("high"))
    dve.wait_ge(dve.last_sem, dve.last_count)
    gains = g.vec(f"norm_g{l}").rearrange("p (i k) -> p i k", i=3)
    for i in range(3):
        for s in range(STREAMS):
            scale = g.mod[:, 3 * i + 1, :, s]
            v.scalar_tensor_tensor(scale, scale, 1.0, gains[:, i, :], ALU.add, ALU.mult).then_inc(g.sem["vec_step"], dve.adds("vec_step"))
    for i in (0, 2):
        gate = g.mod[:, 3 * i + 2, :, :]
        v.tensor_scalar(gate, gate, 0.5, None, ALU.mult).then_inc(g.sem["vec_step"], dve.adds("vec_step"))
    dve.wait_ge(dve.last_sem, dve.last_count)


def modulated_norm_scalar(act, i, width):
    g, nc = act.g, act.g.nc
    h_written(act)
    rms_scalar(act, [g.h[:, k, 0:width] for k in range(KT)], width, D)
    for k in range(KT):
        act.wait_ge(g.sem["scaled"], act.due("scaled"))
        for s in range(width // TOK):
            part = g.xn[:, k, s * TOK:(s + 1) * TOK]
            ins = nc.scalar.activation(part, part, ACT.Identity, bias=g.mod[:, 3 * i, k, s:s + 1])
            if s == width // TOK - 1:
                ins.then_inc(g.sem["shifted"], act.adds("shifted"))
            else:
                ins.then_inc(g.sem["act_step"], act.adds("act_step"))


def modulated_norm_vector(dve, i, width):
    g, nc = dve.g, dve.g.nc
    rms_vector(dve, width)
    for k in range(KT):
        for s in range(width // TOK):
            cols = slice(s * TOK, (s + 1) * TOK)
            ins = nc.vector.scalar_tensor_tensor(g.xn[:, k, cols], g.h[:, k, cols], g.mod[:, 3 * i + 1, k, s:s + 1],
                                                 g.rinv[:, cols], ALU.mult, ALU.mult)
            if s == width // TOK - 1:
                ins.then_inc(g.sem["scaled"], dve.adds("scaled"))
            else:
                ins.then_inc(g.sem["vec_step"], dve.adds("vec_step"))


def gated_residual(dve, i, width):
    g = dve.g

    def add(j, tile, side):
        for s in range(width // TOK):
            cols = slice(s * TOK, (s + 1) * TOK)
            ins = g.nc.vector.scalar_tensor_tensor(g.h[:, j, cols], tile[:, cols], g.mod[:, 3 * i + 2, j, s:s + 1],
                                                   g.h[:, j, cols], ALU.mult, ALU.add)
            if s == width // TOK - 1:
                ins.then_inc(g.sem[side + "_free"], dve.frees(side))
            else:
                ins.then_inc(g.sem["vec_step"], dve.adds("vec_step"))
    return add


def ffn2_width(kind, l):
    return TOK if kind == "ffn_b" and l == LAYERS - 1 else BOTH


def ffn2_tensor(pe, l, kind):
    width = ffn2_width(kind, l)
    rms_tensor(pe, KT, width)
    ffn_tensor(pe, width)


def ffn2_scalar(act, l, kind):
    g = act.g
    width = ffn2_width(kind, l)
    i = 0 if kind == "ffn_a" else 2
    h_written(act)
    first_splits_scalar(act)
    rms_scalar(act, [g.h[:, k, 0:width] for k in range(KT)], width, D)
    split_input_scalar(act, width, lambda k, s: g.mod[:, 3 * i, k, s:s + 1])
    ffn_scalar(act, width)


def ffn2_vector(dve, l, kind):
    g = dve.g
    width = ffn2_width(kind, l)
    i = 0 if kind == "ffn_a" else 2
    first_splits_vector(dve)
    rms_vector(dve, width)
    split_input_vector(dve, width, lambda k, s: g.mod[:, 3 * i + 1, k, s:s + 1])
    ffn_vector(dve, width, gated_residual(dve, i, width))



DT = BOTH // P
CHUNK_ORDER = ((2, 3, 0, 1), (3, 2, 1, 0))
GH = DN_GROUP
LEVELS = 7


def delta_buffers(g):
    r = regions(g, [
        ("g_tok", (DT, 2, DN_HEADS)),
        ("beta", (DT, 2, DN_HEADS)),
        ("gc", (DT, 2, DN_HEADS)),
        ("gl", (DT, 2, DN_HEADS)),
        ("key_decay", (DT, 2, DN_HEADS)),
        ("tmp_g", (DT, 2, DN_HEADS)),
        ("abs_g", (DT, 2, DN_HEADS)),
        ("neg_rate", (2, DN_HEADS)),
        ("q", (GH, BOTH)), ("k", (GH, BOTH)),
        ("k_tok", (GH, BOTH)), ("v_tok", (GH, BOTH)),
        ("o", (GH, BOTH)),
        ("product", (2, 512)), ("row_decay", (2, 512)), ("scores", (2, 2, 512)), ("q_in", (2, 512)), ("k_in", (2, 512)),
        ("k_out", (2, 512)), ("lower", (2, 512)), ("inv", (2, 512)), ("inv_t", (2, 512)), ("level_a", (2, 512)),
        ("level_b", (2, 512)), ("state", (2, 512)),
    ])
    r["new_v"] = r["product"]
    r["decays"] = g.silu
    r["rest"] = (g.root, g.rinv)
    at = r["arena_at"]
    r["raw"] = g.region(at, 2, STREAMS, TOK + 4)
    r["conv"] = g.region(at + 1040, 2, STREAMS, TOK)
    r["v"] = g.region(at + 1040 + 1024, GH, BOTH)
    return r


def heads_view(ap):
    return ap.rearrange("p (h n) -> p h n", h=GH)


def group_tiles():
    return [(what, h) for what in "qkvz" for h in range(GH)]


def delta_tensor(pe, l, kind):
    g = pe.g
    b = delta_buffers(g)
    tri = g.const("not_before")
    rms_tensor(pe, KT, BOTH)
    pe.wait_ge(g.sem["shifted"], pe.due("shifted", KT))
    pe.wait_ge(g.landed[pe.chunks % SLOTS], 16 * (pe.chunks // SLOTS + 1))
    w = pe.chunk(KT, 32)
    pe.wait_ge(g.sem["high_free"], pe.tiles["high"] - 3)
    tile = pe.open("high")
    for t in range(DT):
        for k in range(KT):
            pe.mm(tile[:, t * 32:(t + 1) * 32], g.xn[:, k, t * P:(t + 1) * P], w[:, k, :], k == 0, k == KT - 1,
                  full="high" if t == DT - 1 and k == KT - 1 else None)
    pe.release()
    pe.wait_ge(g.sem["decay_tok"], pe.due("decay_tok"))
    pe.wait_ge(g.sem["high_free"], pe.tiles["high"] - 3)
    tile = pe.open("high")
    for t in range(DT):
        for d in range(2):
            at = (t * 2 + d) * DN_HEADS
            pe.mm(tile[:, at:at + DN_HEADS], tri[:, d, :], b["g_tok"][:, t, d, :])
    pe.mm(tile[:, 64:128], g.const("ones"), b["g_tok"].rearrange("p t d h -> p (t d h)"), full="high")

    for group in range(DN_HEADS // GH):
        tiles = group_tiles()
        w = None
        for n in range(len(tiles) + 2):
            if n < len(tiles):
                if n % 2 == 0:
                    pe.wait_ge(g.landed[pe.chunks % SLOTS], 16 * (pe.chunks // SLOTS + 1))
                    w = pe.chunk(KT, 256)
                pe.wait_ge(g.sem["high_free"], pe.tiles["high"] - 3)
                tile = pe.open("high")
                for k in range(KT):
                    pe.mm(tile[:, :], w[:, k, (n % 2) * P:(n % 2 + 1) * P], g.xn[:, k, :], k == 0, k == KT - 1,
                          full="high" if k == KT - 1 else None)
                if n % 2:
                    pe.release()
            if 2 <= n < 2 + 2 * GH:
                rms_tensor(pe, 1, BOTH, source=g.silu[:, n % 2, :])
        pe.wait_ge(g.sem["dn_normed"], pe.due("dn_normed", 2 * GH))
        pe.wait_ge(g.sem["dn_act"], pe.due("dn_act", 3 * GH))
        for source in ("k", "v"):
            for h in range(GH):
                pe.wait_ge(g.sem["high_free"], pe.tiles["high"] - 3)
                tile = pe.open("high")
                for t in range(DT):
                    pe.transpose(tile[:, t * P:(t + 1) * P], b[source][:, h, t * P:(t + 1) * P],
                                 full="high" if t == DT - 1 else None)
        for step in range(DT):
            delta_step_tensor(pe, b, group, step)
        for h in range(GH):
            rms_tensor(pe, 1, BOTH, source=g.silu[:, h % 2, :])
    pe.wait_ge(g.sem["mix_done"], pe.due("mix_done", DN_HEADS))
    out_projection(pe, BOTH)


ROWS_AFTER, KEYS_AFTER = 3, 5


def changed_half(ap, level, d, name):
    later = (name == "inv_t") != (d == 1)
    return ap.rearrange("p (b two s) -> p b two s", two=2, s=1 << level)[:, :, int(later), :]


def delta_step_tensor(pe, b, group, step):
    g = pe.g
    tri = g.const("not_before")

    def four(side, lhsT, rhs, accumulate=None):
        pe.wait_ge(g.sem[side + "_free"], pe.tiles[side] - 3)
        tile = pe.open(side)
        for h in range(GH):
            out = tile[:, h * P:(h + 1) * P]
            last = side if h == GH - 1 else None
            if accumulate:
                pe.mm(out, lhsT(h), rhs(h), True, False)
                pe.mm(out, accumulate[0](h), accumulate[1](h), False, True, full=last)
            else:
                pe.mm(out, lhsT(h), rhs(h), full=last)

    def half(side, lhsT, rhs):
        pe.wait_ge(g.sem[side + "_free"], pe.tiles[side] - 3)
        tile = pe.open(side)
        for h in range(GH):
            pe.mm(tile[:, h * (P // 2):(h + 1) * (P // 2)], lhsT(h), rhs(h), full=side if h == GH - 1 else None)

    def part(name, d):
        return lambda h: b[name][:, d, h * P:(h + 1) * P]

    def decay_rows(step):
        for d in range(2):
            four("high", lambda h: b["g_tok"][:, CHUNK_ORDER[d][step], d, group * GH + h:group * GH + h + 1].to_broadcast([P, P]),
                 lambda h: tri[:, d, :])

    def key_products(step, d):
        at = CHUNK_ORDER[d][step] * P
        cols = slice(at, at + P)
        four("high", lambda h: b["k"][:, h, cols], lambda h: b["k"][:, h, cols])
        four("high", lambda h: b["k"][:, h, cols], lambda h: b["q"][:, h, cols])

    following = step + 1 < DT
    if step == 0:
        decay_rows(0)
        key_products(0, 0)
        key_products(0, 1)
    for d in range(2):
        pe.wait_ge(g.sem["inv_start"], pe.due("inv_start"))
        pe.wait_ge(g.sem["low_free"], pe.tiles["low"] - 3)
        tile = pe.open("low")
        for h in range(GH):
            pe.transpose(tile[:, h * P:(h + 1) * P], b["inv_t"][:, d, h * P:(h + 1) * P], full="low" if h == GH - 1 else None)
    for level in range(1, LEVELS):
        masked = "level_b" if level % 2 else "level_a"
        for d in range(2):
            pe.wait_ge(g.sem["low_free"], pe.tiles["low"] - 1)
            pe.wait_ge(g.sem["masked"], pe.due("masked"))
            if level > 1:
                ahead = 2 if following and level - 1 in (ROWS_AFTER, KEYS_AFTER) else 0
                pe.wait_ge(g.sem["high_free"], pe.tiles["high"] - ahead - (2 - 2 * d))
            four("low", part(masked, d), part("inv", d))
        for d in range(2):
            pe.wait_ge(g.sem["low_free"], pe.tiles["low"] - (1 - d))
            if level < LEVELS - 1:
                half("high", part("inv_t", d), lambda h: changed_half(b["product"][:, d, h * P:(h + 1) * P], level, d, "inv"))
            half("high", part("product", d), lambda h: changed_half(b["inv_t"][:, d, h * P:(h + 1) * P], level, d, "inv_t"))
        if following and level == ROWS_AFTER:
            decay_rows(step + 1)
        if following and level == KEYS_AFTER:
            key_products(step + 1, 0)
    for d in range(2):
        if step:
            pe.wait_ge(g.sem["state_done"], pe.due("state_done"))
        four("high", part("k_in", d), part("state", d))
    if following:
        key_products(step + 1, 1)
    for d in range(2):
        pe.wait_ge(g.sem["high_free"], pe.tiles["high"] - (2 if following else 0) - (1 - d))
        four("low", part("inv_t", d), lambda h: b["rest"][d][:, h * P:(h + 1) * P])
    for d in range(2):
        pe.wait_ge(g.sem["low_free"], pe.tiles["low"] - (1 - d))
        four("high", part("k_out", d), part("new_v", d))
        four("high", part("new_v", d), lambda h: b["scores"][:, step % 2, d, h * P:(h + 1) * P],
             (part("state", d), part("q_in", d)))


def delta_scalar(act, l, kind):
    g, nc = act.g, act.g.nc
    A = nc.scalar.activation
    b = delta_buffers(g)
    modulated_norm_scalar(act, 1, BOTH)
    A(b["neg_rate"], g.vec("dn_a_log").rearrange("p (d h) -> p d h", d=2), ACT.Exp).then_inc(g.sem["rate"], act.adds("rate"))
    act.wait_ge(g.sem["gate_abs"], act.due("gate_abs"))
    A(b["abs_g"], b["abs_g"], ACT.Exp, scale=-1.0).then_inc(g.sem["act_step"], act.adds("act_step"))
    act.wait_ge(act.last_sem, act.last_count)
    A(b["abs_g"], b["abs_g"], ACT.Ln, bias=1.0).then_inc(g.sem["act_step"], act.adds("act_step"))
    A(b["beta"], b["beta"], ACT.Sigmoid).then_inc(g.sem["gate_ln"], act.adds("gate_ln"))
    act.skip("high", 2)
    act.wait_ge(g.sem["decay_col"], act.due("decay_col"))
    A(b["key_decay"], b["key_decay"], ACT.Exp).then_inc(g.sem["act_step"], act.adds("act_step"))
    A(b["gl"], b["gl"], ACT.Exp).then_inc(g.sem["gate_exp"], act.adds("gate_exp"))

    for group in range(DN_HEADS // GH):
        tiles = group_tiles()
        for n in range(len(tiles) + 2):
            if n < len(tiles):
                what, h = tiles[n]
                act.wait_ge(g.sem["high_full"], act.tiles["high"] + 1)
                tile = act.tile("high")
                if what == "z":
                    A(g.sq[:, group * GH + h, :], tile[:, :], ACT.Silu).then_inc(g.sem["high_free"], act.frees("high"))
                else:
                    if n < 2:
                        act.wait_ge(g.sem["pads"], act.due("pads"))
                    A(b["raw"][:, n % 2, :, 2:2 + TOK], tile[:, :].rearrange("p (s t) -> p s t", s=STREAMS),
                               ACT.Copy).then_inc(g.sem["high_free"], act.frees("high"))
            if 1 <= n <= 3 * GH:
                what, h = tiles[n - 1]
                act.wait_ge(g.sem["conv_out"], act.due("conv_out"))
                A(b[what][:, h, :].rearrange("p (s t) -> p s t", s=STREAMS), b["conv"][:, (n - 1) % 2, :, :],
                             ACT.Silu).then_inc(g.sem["dn_act"], act.adds("dn_act"))
                if what in "qk":
                    act.wait_ge(act.last_sem, act.last_count)
                    A(g.silu[:, (n - 1) % 2, :], b[what][:, h, :], ACT.Square).then_inc(g.sem["squares"], act.adds("squares"))
            if 2 <= n < 2 + 2 * GH:
                length_root(act, 1.0)
        for source in ("k_tok", "v_tok"):
            for h in range(GH):
                act.wait_ge(g.sem["high_full"], act.tiles["high"] + 1)
                A(b[source][:, h, :], act.tile("high")[:, :], ACT.Copy).then_inc(g.sem["high_free"], act.frees("high"))
        for step in range(DT):
            delta_step_scalar(act, b, group, step)
        act.wait_ge(g.sem["out_done"], act.due("out_done"))
        for h in range(GH):
            A(g.silu[:, h % 2, :], b["o"][:, h, :], ACT.Square).then_inc(g.sem["squares"], act.adds("squares"))
            length_root(act, 1.0 / P)
    act.skip("high", KT)


def length_root(act, scale):
    g = act.g
    act.wait_ge(g.sem["low_free"], act.freed["low"])
    act.wait_ge(g.sem["low_full"], act.tiles["low"] + 1)
    tile = act.tile("low", peek=True)
    act.other_frees("low")
    g.nc.scalar.activation(g.root[:, :], tile[:, :], ACT.Sqrt, scale=scale, bias=g.eps[:, 0:1]).then_inc(g.sem["root"], act.adds("root"))


def delta_step_scalar(act, b, group, step):
    g, nc = act.g, act.g.nc
    A = nc.scalar.activation
    following = step + 1 < DT

    def row_decays():
        act.wait_ge(g.sem["high_free"], act.freed["high"])
        for d in range(2):
            act.wait_ge(g.sem["high_full"], act.tiles["high"] + 1)
            tile = act.tile("high", peek=True)
            act.other_frees("high")
            A(b["row_decay"][:, d, :], tile[:, :], ACT.Exp).then_inc(g.sem["row_decay"], act.adds("row_decay"))
        return act.freed["high"]

    def decays(written):
        for d in range(2):
            act.wait_ge(g.sem["high_free"], written - 1 + d)
            A(b["decays"][:, d, :], b["decays"][:, d, :], ACT.Exp).then_inc(g.sem["decay"], act.adds("decay"))

    if step == 0:
        decays(row_decays())
        act.skip("high", 4)
    for d in range(2):
        act.wait_ge(g.sem["low_full"], act.tiles["low"] + 1)
        A(b["inv"][:, d, :], act.tile("low")[:, :], ACT.Copy).then_inc(g.sem["low_free"], act.frees("low"))
    for level in range(1, LEVELS):
        for d in range(2):
            act.wait_ge(g.sem["low_full"], act.tiles["low"] + 1)
            A(b["product"][:, d, :], act.tile("low")[:, :], ACT.Copy).then_inc(g.sem["low_free"], act.frees("low"))
        if following and level == ROWS_AFTER + 1:
            decays(written)
        act.skip("high", 4 if level < LEVELS - 1 else 2)
        if following and level == ROWS_AFTER:
            written = row_decays()
        if following and level == KEYS_AFTER:
            act.skip("high", 2)
    act.skip("high", 4 if following else 2)
    for d in range(2):
        act.wait_ge(g.sem["low_full"], act.tiles["low"] + 1)
        tile = act.tile("low")
        for h in range(GH):
            ins = A(b["new_v"][:, d, h * P:(h + 1) * P], tile[:, h * P:(h + 1) * P], ACT.Copy,
                    scale=b["beta"][:, CHUNK_ORDER[d][step], d, group * GH + h:group * GH + h + 1])
            if h == GH - 1:
                ins.then_inc(g.sem["low_free"], act.frees("low"))
            else:
                ins.then_inc(g.sem["act_step"], act.adds("act_step"))
    act.skip("high", 4)


def delta_vector(dve, l, kind):
    g, nc = dve.g, dve.g.nc
    v = nc.vector
    b = delta_buffers(g)
    modulated_norm_vector(dve, 1, BOTH)
    dve.wait_ge(g.sem["high_full"], dve.tiles["high"] + 1)
    tile = dve.tile("high")
    source = tile[:, 0:DT * 32].rearrange("p (t d w h) -> p t d w h", t=DT, d=2, w=2)
    bias = g.vec("dn_dt_bias").rearrange("p (d h) -> p d h", d=2)
    for t in range(DT):
        v.tensor_tensor(b["tmp_g"][:, t, :, :], source[:, t, :, 0, :], bias, ALU.add).then_inc(g.sem["vec_step"], dve.adds("vec_step"))
    for t in range(DT):
        ins = v.tensor_copy(b["beta"][:, t, :, :], source[:, t, :, 1, :])
        if t == DT - 1:
            ins.then_inc(g.sem["high_free"], dve.frees("high"))
        else:
            ins.then_inc(g.sem["vec_step"], dve.adds("vec_step"))
    dve.wait_ge(dve.last_sem, dve.last_count)
    v.scalar_tensor_tensor(b["abs_g"], b["tmp_g"], -1.0, b["tmp_g"], ALU.mult, ALU.max).then_inc(g.sem["gate_abs"], dve.adds("gate_abs"))
    dve.wait_ge(g.sem["rate"], dve.due("rate"))
    v.tensor_scalar(b["neg_rate"], b["neg_rate"], -1.0, None, ALU.mult).then_inc(g.sem["vec_step"], dve.adds("vec_step"))
    dve.wait_ge(g.sem["gate_ln"], dve.due("gate_ln"))
    v.scalar_tensor_tensor(b["tmp_g"], b["tmp_g"], 0.0, b["abs_g"], ALU.max, ALU.add).then_inc(g.sem["vec_step"], dve.adds("vec_step"))
    dve.wait_ge(dve.last_sem, dve.last_count)
    for t in range(DT):
        ins = v.tensor_tensor(b["g_tok"][:, t, :, :], b["tmp_g"][:, t, :, :], b["neg_rate"], ALU.mult)
        if t == DT - 1:
            ins.then_inc(g.sem["decay_tok"], dve.adds("decay_tok"))
        else:
            ins.then_inc(g.sem["vec_step"], dve.adds("vec_step"))
    dve.wait_ge(g.sem["high_full"], dve.tiles["high"] + 1)
    tile = dve.tile("high")
    flat = lambda name: b[name].rearrange("p t d h -> p (t d h)")
    v.tensor_copy(flat("gc"), tile[:, 0:64]).then_inc(g.sem["vec_step"], dve.adds("vec_step"))
    v.tensor_copy(flat("gl"), tile[:, 64:128]).then_inc(g.sem["vec_step"], dve.adds("vec_step"))
    dve.wait_ge(dve.last_sem, dve.last_count)
    v.tensor_tensor(flat("key_decay"), tile[:, 64:128], flat("gc"), ALU.subtract).then_inc(g.sem["high_free"], dve.frees("high"))
    dve.wait_ge(dve.last_sem, dve.last_count)
    v.tensor_scalar(flat("gc"), flat("gc"), -1.0, None, ALU.mult).then_inc(g.sem["decay_col"], dve.adds("decay_col"))
    dve.wait_ge(g.sem["gate_exp"], dve.due("gate_exp"))

    taps = g.vec("dn_conv")
    for group in range(DN_HEADS // GH):
        tiles = group_tiles()
        for n in range(2):
            for at in (0, TOK + 2):
                ins = v.memset(b["raw"][:, n, :, at:at + 2], 0.0)
                if at:
                    ins.then_inc(g.sem["pads"], dve.adds("pads"))
                else:
                    ins.then_inc(g.sem["vec_step"], dve.adds("vec_step"))
        for n in range(len(tiles)):
            if 2 <= n < 2 + 2 * GH:
                length_apply(dve, b, *tiles[n - 2])
            if n < 3 * GH:
                what, h = tiles[n]
                if n >= 2:
                    dve.wait_ge(g.sem["dn_act"], dve.due("dn_act"))
                dve.skip("high")
                dve.wait_ge(g.sem["high_free"], dve.freed["high"])
                tap = ("qkv".index(what) * DN_HEADS + group * GH + h) * DN_CONV
                x, out = b["raw"][:, n % 2, :, :], b["conv"][:, n % 2, :, :]
                v.tensor_scalar(out, x[:, :, 0:TOK], taps[:, tap:tap + 1], None, ALU.mult).then_inc(g.sem["vec_step"], dve.adds("vec_step"))
                for k in range(1, DN_CONV):
                    dve.wait_ge(dve.last_sem, dve.last_count)
                    ins = v.scalar_tensor_tensor(out, x[:, :, k:k + TOK], taps[:, tap + k:tap + k + 1], out,
                                                 ALU.mult, ALU.add)
                    if k < DN_CONV - 1:
                        ins.then_inc(g.sem["vec_step"], dve.adds("vec_step"))
                    else:
                        ins.then_inc(g.sem["conv_out"], dve.adds("conv_out"))
            else:
                dve.skip("high")
        dve.wait_ge(g.sem["dn_act"], dve.due("dn_act", 2))
        dve.skip("high", 2 * GH)
        dve.wait_ge(g.sem["high_free"], dve.freed["high"])
        v.memset(b["state"], 0.0).then_inc(g.sem["vec_step"], dve.adds("vec_step"))
        v.memset(b["o"], 0.0).then_inc(g.sem["vec_step"], dve.adds("vec_step"))
        dve.wait_ge(dve.last_sem, dve.last_count)
        for step in range(DT):
            delta_step_vector(dve, b, group, step)
        dve.skip("low", DT * 2 * (1 + (LEVELS - 1) + 1))
        dve.wait_ge(dve.last_sem, dve.last_count)
        v.tensor_copy(b["tmp_g"][:, 0, 0, 0:1], b["o"][:, 0, 0:1]).then_inc(g.sem["out_done"], dve.adds("out_done"))
        for h in range(GH):
            rms_vector(dve, BOTH)
            v.scalar_tensor_tensor(b["o"][:, h, :], b["o"][:, h, :], g.vec("dn_o_gain"), g.rinv[:, :],
                                            ALU.mult, ALU.mult).then_inc(g.sem["vec_step"], dve.adds("vec_step"))
            dve.wait_ge(dve.last_sem, dve.last_count)
            y = g.sq[:, group * GH + h, :]
            v.tensor_tensor(y, y, b["o"][:, h, :], ALU.mult).then_inc(g.sem["mix_done"], dve.adds("mix_done"))
    add = gated_residual(dve, 1, BOTH)
    for j in range(KT):
        dve.wait_ge(g.sem["high_full"], dve.tiles["high"] + 1)
        add(j, dve.tile("high"), "high")


def length_apply(dve, b, what, h):
    g, nc = dve.g, dve.g.nc
    rms_vector(dve, BOTH)
    nc.vector.scalar_tensor_tensor(b[what][:, h, :], b[what][:, h, :], P ** -0.5 if what == "q" else 1.0,
                                              g.rinv[:, :], ALU.mult, ALU.mult).then_inc(g.sem["dn_normed"], dve.adds("dn_normed"))


def delta_step_vector(dve, b, group, step):
    g, nc = dve.g, dve.g.nc
    v = nc.vector
    masks = g.const("levels")
    following = step + 1 < DT

    def col(name, step, d, h):
        return b[name][:, CHUNK_ORDER[d][step], d, group * GH + h:group * GH + h + 1]

    def chunk_cols(step, d):
        return slice(CHUNK_ORDER[d][step] * P, (CHUNK_ORDER[d][step] + 1) * P)

    def all_heads(mask):
        return mask.rearrange("p (o n) -> p o n", o=1).to_broadcast([P, GH, P])

    def each(op, finish):
        for h in range(GH):
            ins = op(h, slice(h * P, (h + 1) * P))
            if h == GH - 1:
                finish(ins)
            else:
                ins.then_inc(g.sem["vec_step"], dve.adds("vec_step"))

    def log_decays(step):
        for d in range(2):
            dve.wait_ge(g.sem["high_full"], dve.tiles["high"] + 1)
            tile = dve.tile("high")
            dve.wait_ge(g.sem["row_decay"], dve.due("row_decay"))
            each(lambda h, c: v.tensor_scalar(b["decays"][:, d, c], tile[:, c], col("gc", step, d, h), 0.0, ALU.add, ALU.min),
                 lambda ins: ins.then_inc(g.sem["high_free"], dve.frees("high")))

    def lower_and_scores(step, d):
        dve.wait_ge(g.sem["high_full"], dve.tiles["high"] + 1)
        kk = dve.tile("high")
        dve.wait_ge(g.sem["high_full"], dve.tiles["high"] + 1)
        kq = dve.tile("high")
        dve.wait_ge(g.sem["decay"], dve.due("decay"))
        v.tensor_tensor(heads_view(b["decays"][:, d, :]), heads_view(b["decays"][:, d, :]),
                        all_heads(g.const("not_before")[:, d, :]), ALU.mult).then_inc(g.sem["vec_step"], dve.adds("vec_step"))
        dve.wait_ge(dve.last_sem, dve.last_count)
        each(lambda h, c: v.scalar_tensor_tensor(b["lower"][:, d, c], kk[:, c], col("beta", step, d, h),
                                                 b["decays"][:, d, c], ALU.mult, ALU.mult),
             lambda ins: ins.then_inc(g.sem["high_free"], dve.frees("high")))
        v.tensor_tensor(b["scores"][:, step % 2, d, :], kq[:, :], b["decays"][:, d, :], ALU.mult).then_inc(g.sem["high_free"], dve.frees("high"))
        dve.wait_ge(dve.last_sem, dve.last_count)
        v.tensor_tensor(heads_view(b["level_b"][:, d, :]), heads_view(b["lower"][:, d, :]),
                        all_heads(masks[:, 1, :]), ALU.mult).then_inc(g.sem["masked"], dve.adds("masked"))

    def first_level():
        for d in range(2):
            v.tensor_tensor(heads_view(b["level_a"][:, d, :]), heads_view(b["lower"][:, d, :]),
                            all_heads(masks[:, 0, :]), ALU.mult).then_inc(g.sem["vec_step"], dve.adds("vec_step"))

    def state_operand(n):
        d = n % 2
        cols, row = chunk_cols(step, d), heads_view(b["row_decay"][:, d, :])
        if n < 2:
            v.tensor_tensor(heads_view(b["q_in"][:, d, :]), b["q"][:, :, cols], row, ALU.mult).then_inc(g.sem["vec_step"], dve.adds("vec_step"))
        elif n < 4:
            v.tensor_tensor(heads_view(b["k_in"][:, d, :]), b["k"][:, :, cols], row, ALU.mult).then_inc(g.sem["vec_step"], dve.adds("vec_step"))
        else:
            each(lambda h, c: v.tensor_scalar(b["k_out"][:, d, c], b["k_tok"][:, h, cols], col("key_decay", step, d, h), None,
                                              ALU.mult), lambda ins: ins.then_inc(g.sem["vec_step"], dve.adds("vec_step")))

    if step == 0:
        log_decays(0)
        lower_and_scores(0, 0)
        lower_and_scores(0, 1)
        first_level()
    dve.wait_ge(dve.last_sem, dve.last_count)
    for d in range(2):
        v.scalar_tensor_tensor(heads_view(b["inv_t"][:, d, :]), heads_view(b["level_a"][:, d, :]), -1.0,
                               all_heads(g.const("identity")), ALU.mult, ALU.add).then_inc(g.sem["inv_start"], dve.adds("inv_start"))
    operands = {1: (0, 1), 2: (2, 3), 3: (4,), 4: (5,)}
    for level in range(1, LEVELS):
        if level < LEVELS - 1:
            masked = "level_a" if level % 2 else "level_b"
            dve.wait_ge(dve.last_sem, dve.last_count)
            for d in range(2):
                v.tensor_tensor(heads_view(b[masked][:, d, :]), heads_view(b["lower"][:, d, :]),
                                all_heads(masks[:, level + 1, :]), ALU.mult).then_inc(g.sem["masked"], dve.adds("masked"))
        for d in range(2):
            for name in (("inv", "inv_t") if level < LEVELS - 1 else ("inv_t",)):
                dve.wait_ge(g.sem["high_full"], dve.tiles["high"] + 1)
                tile = dve.tile("high")
                changed = changed_half(b[name][:, d, :], level, d, name)
                v.tensor_tensor(changed, changed, tile[:, 0:GH * P // 2].rearrange("p (b s) -> p b s", s=1 << level),
                                ALU.subtract).then_inc(g.sem["high_free"], dve.frees("high"))
        for n in operands.get(level, ()):
            state_operand(n)
        if following and level == ROWS_AFTER:
            log_decays(step + 1)
        if following and level == KEYS_AFTER:
            lower_and_scores(step + 1, 0)
    for d in range(2):
        dve.wait_ge(g.sem["high_full"], dve.tiles["high"] + 1)
        tile = dve.tile("high")
        v.tensor_tensor(heads_view(b["rest"][d][:, :]), b["v_tok"][:, :, chunk_cols(step, d)], heads_view(tile[:, :]),
                        ALU.subtract).then_inc(g.sem["high_free"], dve.frees("high"))
    if following:
        lower_and_scores(step + 1, 1)
        first_level()
    for d in range(2):
        dve.wait_ge(g.sem["high_full"], dve.tiles["high"] + 1)
        key_values = dve.tile("high")
        dve.wait_ge(g.sem["high_full"], dve.tiles["high"] + 1)
        out = dve.tile("high")
        each(lambda h, c: v.scalar_tensor_tensor(b["state"][:, d, c], b["state"][:, d, c], col("gl", step, d, h),
                                                 key_values[:, c], ALU.mult, ALU.add),
             lambda ins: ins.then_inc(g.sem["high_free"], dve.frees("high")))
        o = b["o"][:, :, chunk_cols(step, d)]
        v.tensor_tensor(o, o, heads_view(out[:, :]), ALU.add).then_inc(g.sem["high_free"], dve.frees("high"))
        if following:
            dve.wait_ge(dve.last_sem, dve.last_count)
            v.tensor_copy(b["tmp_g"][:, 0, 0, 0:1], b["state"][:, d, 0:1]).then_inc(g.sem["state_done"], dve.adds("state_done"))



PAIRS = SWA_HEADS // 2
KEY_TILES = BOTH // P
SWA_SCALE = SWA_DIM ** -0.5


def swa_buffers(g):
    return regions(g, [
        ("q", (PAIRS, TOK)),
        ("k", (SWA_KV // 2, BOTH)),
        ("v", (KEY_TILES, SWA_KV * SWA_DIM)),
        ("tmp", (2, TOK)),
        ("probs", (2, 4, BOTH)),
        ("probs_t", (2, KEY_TILES, TOK)),
        ("peak", (2, 4)), ("neg_peak", (2, 4)), ("sink", (2, 4)), ("total", (2, 4)),
    ])


def swa_tensor(pe, l, kind):
    g = pe.g
    b = swa_buffers(g)
    rms_tensor(pe, KT, BOTH)
    pe.wait_ge(g.sem["shifted"], pe.due("shifted", KT))
    for _ in range(PAIRS // 2):
        pe.wait_ge(g.landed[pe.chunks % SLOTS], 16 * (pe.chunks // SLOTS + 1))
        w = pe.chunk(KT, 256)
        for m in range(2):
            pe.wait_ge(g.sem["low_free"], pe.tiles["low"] - 3)
            tile = pe.open("low")
            for k in range(KT):
                pe.mm(tile[:, 0:TOK], w[:, k, m * P:(m + 1) * P], g.xn[:, k, 0:TOK], k == 0, k == KT - 1,
                      full="low" if k == KT - 1 else None)
        pe.release()
    pe.wait_ge(g.landed[pe.chunks % SLOTS], 16 * (pe.chunks // SLOTS + 1))
    w = pe.chunk(KT, 256)
    for m in range(2):
        pe.wait_ge(g.sem["low_free"], pe.tiles["low"] - 3)
        tile = pe.open("low")
        for k in range(KT):
            pe.mm(tile[:, :], w[:, k, m * P:(m + 1) * P], g.xn[:, k, :], k == 0, k == KT - 1,
                  full="low" if k == KT - 1 else None)
    pe.release()
    pe.wait_ge(g.landed[pe.chunks % SLOTS], 16 * (pe.chunks // SLOTS + 1))
    w = pe.chunk(KT, 256)
    for t in range(KEY_TILES):
        pe.wait_ge(g.sem["low_free"], pe.tiles["low"] - 3)
        tile = pe.open("low")
        for k in range(KT):
            pe.mm(tile[:, 0:256], g.xn[:, k, t * P:(t + 1) * P], w[:, k, :], k == 0, k == KT - 1,
                  full="low" if k == KT - 1 else None)
    pe.release()
    for n in range(PAIRS // 2 + 2):
        rms_tensor(pe, 1, BOTH, "head_ones", source=g.silu[:, n % 2, :])
    pe.wait_ge(g.sem["dn_normed"], pe.due("dn_normed", PAIRS + 2))
    for n in range(PAIRS // 2):
        pe.wait_ge(g.sem["high_free"], pe.tiles["high"] - 3)
        tile = pe.open("high")
        pe.mm(tile[:, :], g.const("rotate"), b["q"][:, 2 * n:2 * n + 2, :], full="high")
    pe.wait_ge(g.sem["high_free"], pe.tiles["high"] - 3)
    tile = pe.open("high")
    pe.mm(tile[:, :], g.const("rotate"), b["k"][:, :, 0:TOK], full="high")
    pe.wait_ge(g.sem["rotated"], pe.due("rotated", PAIRS + 2))

    def scores(p):
        for i, head in enumerate(swa_pairs()[p]):
            base, kv = SWA_DIM * i, head // (SWA_HEADS // SWA_KV)
            for q in range(2):
                pe.wait_ge(g.sem["low_free"], pe.tiles["low"] - 3)
                tile = pe.open("low")
                far = 1 - q
                pe.mm(tile[:, :], b["q"][base:base + SWA_DIM, p, q * P:(q + 1) * P], b["k"][base:base + SWA_DIM, kv // 2, :],
                      True, False)
                pe.mm(tile[:, far * P:(far + 1) * P], g.const("identity"), g.const("swa_mask")[:, q, far * P:(far + 1) * P],
                      False, True, full="low")

    scores(0)
    for p in range(PAIRS):
        if p + 1 < PAIRS:
            scores(p + 1)
        pe.wait_ge(g.sem["probs_scaled"], pe.due("probs_scaled", 4))
        for i in range(2):
            for half in range(2):
                pe.wait_ge(g.sem["high_free"], pe.tiles["high"] - 3)
                tile = pe.open("high")
                for t in range(2):
                    for q in range(2):
                        key = half * 2 + t
                        pe.transpose(tile[:, t * TOK + q * P:t * TOK + (q + 1) * P],
                                     b["probs"][:, p % 2, i * 2 + q, key * P:(key + 1) * P],
                                     full="high" if t and q else None)
        pe.wait_ge(g.sem["high_free"], pe.tiles["high"])
        pe.wait_ge(g.sem["high_free"], pe.tiles["high"] - 3)
        tile = pe.open("high")
        for i, head in enumerate(swa_pairs()[p]):
            kv = head // (SWA_HEADS // SWA_KV)
            for t in range(KEY_TILES):
                pe.mm(tile[SWA_DIM * i:SWA_DIM * (i + 1), 0:TOK], b["v"][:, t, kv * SWA_DIM:(kv + 1) * SWA_DIM],
                      b["probs_t"][:, i, t, :], t == 0, t == KEY_TILES - 1,
                      full="high" if i and t == KEY_TILES - 1 else None)
    pe.wait_ge(g.sem["high_free"], pe.tiles["high"])
    out_projection(pe, TOK)


def swa_scalar(act, l, kind):
    g, nc = act.g, act.g.nc
    A = nc.scalar.activation
    b = swa_buffers(g)
    modulated_norm_scalar(act, 1, BOTH)
    for p in range(PAIRS):
        act.wait_ge(g.sem["low_full"], act.tiles["low"] + 1)
        A(b["q"][:, p, :], act.tile("low")[:, 0:TOK], ACT.Copy).then_inc(g.sem["low_free"], act.frees("low"))
    for m in range(2):
        act.wait_ge(g.sem["low_full"], act.tiles["low"] + 1)
        A(b["k"][:, m, :], act.tile("low")[:, :], ACT.Copy).then_inc(g.sem["low_free"], act.frees("low"))
    for t in range(KEY_TILES):
        act.wait_ge(g.sem["low_full"], act.tiles["low"] + 1)
        A(b["v"][:, t, :], act.tile("low")[:, 0:256], ACT.Copy).then_inc(g.sem["low_free"], act.frees("low"))
    act.wait_ge(act.last_sem, act.last_count)
    for n in range(PAIRS // 2 + 2):
        source = b["q"][:, 2 * n:2 * n + 2, :] if n < PAIRS // 2 else b["k"][:, n - PAIRS // 2, :]
        into = g.silu[:, n % 2, :]
        A(into.rearrange("p (a t) -> p a t", a=2) if n < PAIRS // 2 else into, source, ACT.Square).then_inc(g.sem["squares"], act.adds("squares"))
        length_root(act, 1.0 / SWA_DIM)
    act.skip("high", PAIRS // 2 + 1)
    for p in range(PAIRS):
        act.wait_ge(g.sem["neg_max"], act.due("neg_max"))
        A(b["sink"][:, p % 2, :], b["sink"][:, p % 2, :], ACT.Exp).then_inc(g.sem["sink_exp"], act.adds("sink_exp"))
        for n in range(4):
            act.wait_ge(g.sem["low_full"], act.tiles["low"] + 1)
            tile = act.tile("low")
            A(b["probs"][:, p % 2, n, :], tile[:, :], ACT.Exp, scale=SWA_SCALE,
                       bias=b["neg_peak"][:, p % 2, n:n + 1], accum_out=b["total"][:, p % 2, n:n + 1]).then_inc(g.sem["low_free"], act.frees("low"))
    act.skip("high", 5 * PAIRS + KT)


def swa_vector(dve, l, kind):
    g, nc = dve.g, dve.g.nc
    v = nc.vector
    b = swa_buffers(g)
    modulated_norm_vector(dve, 1, BOTH)
    dve.skip("low", PAIRS + 2 + KEY_TILES)
    for n in range(PAIRS // 2 + 2):
        rms_vector(dve, BOTH)
        for half in range(2):
            if n < PAIRS // 2:
                part, gain = b["q"][:, 2 * n + half, :], g.vec("swa_q_gain")
            else:
                part, gain = b["k"][:, n - PAIRS // 2, half * TOK:(half + 1) * TOK], g.vec("swa_k_gain")
            ins = v.scalar_tensor_tensor(part, part, gain, g.rinv[:, half * TOK:(half + 1) * TOK], ALU.mult, ALU.mult)
            if n < PAIRS // 2 or half:
                ins.then_inc(g.sem["dn_normed"], dve.adds("dn_normed"))
            else:
                ins.then_inc(g.sem["vec_step"], dve.adds("vec_step"))
    cos, sin = g.const("swa_cos"), g.const("swa_sin")
    for n in range(PAIRS // 2 + 1):
        dve.wait_ge(g.sem["high_full"], dve.tiles["high"] + 1)
        tile = dve.tile("high")
        for half in range(2):
            raw = b["q"][:, 2 * n + half, :] if n < PAIRS // 2 else b["k"][:, half, 0:TOK]
            tmp = b["tmp"][:, half, :]
            v.tensor_tensor(raw, raw, cos, ALU.mult).then_inc(g.sem["vec_step"], dve.adds("vec_step"))
            ins = v.tensor_tensor(tmp, tile[:, half * TOK:(half + 1) * TOK], sin, ALU.mult)
            if half:
                ins.then_inc(g.sem["high_free"], dve.frees("high"))
            else:
                ins.then_inc(g.sem["vec_step"], dve.adds("vec_step"))
        dve.wait_ge(dve.last_sem, dve.last_count)
        for half in range(2):
            raw = b["q"][:, 2 * n + half, :] if n < PAIRS // 2 else b["k"][:, half, 0:TOK]
            v.tensor_tensor(raw, raw, b["tmp"][:, half, :], ALU.add).then_inc(g.sem["rotated"], dve.adds("rotated"))
        dve.wait_ge(dve.last_sem, dve.last_count)

    def softmax_peak(p):
        for n in range(4):
            dve.wait_ge(g.sem["low_full"], dve.tiles["low"] + 1)
            tile = dve.tile("low", peek=True)
            dve.other_frees("low")
            v.reduce_max(b["peak"][:, p % 2, n:n + 1], tile[:, :], AX).then_inc(g.sem["vec_step"], dve.adds("vec_step"))
        dve.wait_ge(dve.last_sem, dve.last_count)
        sink = g.vec("sink")[:, 4 * p:4 * p + 4]
        v.scalar_tensor_tensor(b["peak"][:, p % 2, :], b["peak"][:, p % 2, :], SWA_SCALE, sink, ALU.mult, ALU.max).then_inc(g.sem["vec_step"], dve.adds("vec_step"))
        dve.wait_ge(dve.last_sem, dve.last_count)
        v.tensor_scalar(b["neg_peak"][:, p % 2, :], b["peak"][:, p % 2, :], -1.0, None, ALU.mult).then_inc(g.sem["vec_step"], dve.adds("vec_step"))
        v.tensor_tensor(b["sink"][:, p % 2, :], sink, b["peak"][:, p % 2, :], ALU.subtract).then_inc(g.sem["neg_max"], dve.adds("neg_max"))

    softmax_peak(0)
    for p in range(PAIRS):
        dve.wait_ge(g.sem["sink_exp"], dve.due("sink_exp"))
        dve.wait_ge(g.sem["low_free"], dve.freed["low"])
        v.tensor_tensor(b["total"][:, p % 2, :], b["total"][:, p % 2, :], b["sink"][:, p % 2, :], ALU.add).then_inc(g.sem["vec_step"], dve.adds("vec_step"))
        dve.wait_ge(dve.last_sem, dve.last_count)
        v.reciprocal(b["total"][:, p % 2, :], b["total"][:, p % 2, :]).then_inc(g.sem["vec_step"], dve.adds("vec_step"))
        dve.wait_ge(dve.last_sem, dve.last_count)
        for n in range(4):
            v.tensor_scalar(b["probs"][:, p % 2, n, :], b["probs"][:, p % 2, n, :],
                                       b["total"][:, p % 2, n:n + 1], None, ALU.mult).then_inc(g.sem["probs_scaled"], dve.adds("probs_scaled"))
        if p + 1 < PAIRS:
            softmax_peak(p + 1)
        for i in range(2):
            for half in range(2):
                dve.wait_ge(g.sem["high_full"], dve.tiles["high"] + 1)
                tile = dve.tile("high")
                v.tensor_copy(b["probs_t"][:, i, 2 * half:2 * half + 2, :].rearrange("p t q -> p (t q)"),
                                       tile[:, :]).then_inc(g.sem["high_free"], dve.frees("high"))
        dve.wait_ge(g.sem["high_full"], dve.tiles["high"] + 1)
        tile = dve.tile("high")
        v.tensor_copy(g.sq[:, p, 0:TOK], tile[:, 0:TOK]).then_inc(g.sem["high_free"], dve.frees("high"))
    add = gated_residual(dve, 1, TOK)
    for j in range(KT):
        dve.wait_ge(g.sem["high_full"], dve.tiles["high"] + 1)
        add(j, dve.tile("high"), "high")



SETUP = (("ang", (TOK,)), ("turns_i", (TOK,)), ("turns", (TOK,)), ("cos_ang", (TOK,)))


def setup_vector(dve):
    g, nc = dve.g, dve.g.nc
    v = nc.vector
    b = regions(g, SETUP)
    v.memset(g.eps[:, :], EPS).then_inc(g.sem["vec_step"], dve.adds("vec_step"))
    dve.wait_ge(g.sem["tables_in"], dve.due("tables_in", 32))
    dve.wait_ge(g.sem["pos_in"], dve.due("pos_in", 16))
    v.tensor_copy(b["ang"], g.positions).then_inc(g.sem["vec_step"], dve.adds("vec_step"))
    dve.wait_ge(dve.last_sem, dve.last_count)
    v.tensor_scalar(b["ang"], b["ang"], g.vec("inv_freq"), None, ALU.mult).then_inc(g.sem["vec_step"], dve.adds("vec_step"))
    dve.wait_ge(dve.last_sem, dve.last_count)
    whole = g.turns_int
    v.tensor_scalar(whole, b["ang"], 1.0 / TWO_PI, None, ALU.mult).then_inc(g.sem["vec_step"], dve.adds("vec_step"))
    dve.wait_ge(dve.last_sem, dve.last_count)
    v.tensor_copy(b["turns"], whole).then_inc(g.sem["vec_step"], dve.adds("vec_step"))
    dve.wait_ge(dve.last_sem, dve.last_count)
    coarse = 6.28125
    for part in (coarse, TWO_PI - coarse):
        v.scalar_tensor_tensor(b["ang"], b["turns"], -part, b["ang"], ALU.mult, ALU.add).then_inc(g.sem["vec_step"], dve.adds("vec_step"))
        dve.wait_ge(dve.last_sem, dve.last_count)
    v.tensor_scalar(b["cos_ang"], b["ang"], TWO_PI / 4, None, ALU.add).then_inc(g.sem["vec_step"], dve.adds("vec_step"))
    dve.wait_ge(dve.last_sem, dve.last_count)
    v.tensor_scalar(b["turns"], b["cos_ang"], TWO_PI / 2, -TWO_PI, ALU.is_gt, ALU.mult).then_inc(g.sem["vec_step"], dve.adds("vec_step"))
    dve.wait_ge(dve.last_sem, dve.last_count)
    v.tensor_tensor(b["cos_ang"], b["cos_ang"], b["turns"], ALU.add).then_inc(g.sem["vec_step"], dve.adds("vec_step"))
    dve.wait_ge(dve.last_sem, dve.last_count)
    limit = float(np.float32(3.1415925))
    for name in ("ang", "cos_ang"):
        v.tensor_scalar(b[name], b[name], limit, -limit, ALU.min, ALU.max).then_inc(g.sem["rope_angle"], dve.adds("rope_angle"))


def setup_scalar(act):
    g, nc = act.g, act.g.nc
    b = regions(g, SETUP)
    act.wait_ge(g.sem["rope_angle"], act.due("rope_angle", 2))
    nc.scalar.activation(g.rope[:, 1, :], b["ang"], ACT.Sin).then_inc(g.sem["act_step"], act.adds("act_step"))
    nc.scalar.activation(g.rope[:, 0, :], b["cos_ang"], ACT.Sin).then_inc(g.sem["act_step"], act.adds("act_step"))



PROGRAMS = {
    "ffn1": (ffn1_tensor, ffn1_scalar, ffn1_vector),
    "ffn2": (ffn1_tensor, ffn1_scalar, ffn1_vector),
    "mix1": (mix1_tensor, mix1_scalar, mix1_vector),
    "ple": (ple_tensor, ple_scalar, ple_vector),
    "final": (final_tensor, final_scalar, final_vector),
    "ada": (ada_tensor, ada_scalar, ada_vector),
    "ffn_a": (ffn2_tensor, ffn2_scalar, ffn2_vector),
    "ffn_b": (ffn2_tensor, ffn2_scalar, ffn2_vector),
    "delta": (delta_tensor, delta_scalar, delta_vector),
    "swa": (swa_tensor, swa_scalar, swa_vector),
}


def program(nc, xT, ctxT, positions, vectors, consts, weights, out, stages=STAGES):
    total = sum(chunk_count(kind) for kind, _ in stages)
    with ExitStack() as ctx:
        g = Shared(nc, ctx, None)
        g.positions = g.silu[:, 0, 0:TOK].bitcast(I32)
        g.turns_int = g.silu[:, 1, 0:TOK].bitcast(I32)
        block = ctx.enter_context(nc.Block())

        @block.sync
        def _(sync):
            sync.dma_start(g.vectors[:, :], vectors).then_inc(g.sem["tables_in"], 16)
            sync.dma_start(g.consts[:, :], consts).then_inc(g.sem["tables_in"], 16)

            def load(slot, source):
                sync.dma_start(g.ring[:, slot, :], source).then_inc(g.landed[slot], 16)

            for n in range(SLOTS):
                load(n, weights[n])
            trips = (total - SLOTS) // SLOTS
            with sync.Fori(0, trips) as it:
                for s in range(SLOTS):
                    sync.wait_ge(g.sem["weights_used"], it * SLOTS + (s + 1))
                    load(s, weights[it * SLOTS + (SLOTS + s)])
            for n in range(SLOTS * (trips + 1), total):
                sync.wait_ge(g.sem["weights_used"], n - SLOTS + 1)
                load(n % SLOTS, weights[n])
            sync.wait_ge(g.sem["all_done"], 1)
            sync.dma_start(out, g.h[:, :, 0:TOK]).then_inc(g.sem["stream_out"], 16)
            sync.wait_ge(g.sem["stream_out"], 16)

        @block.scalar
        def _(scalar):
            act = Engine(g, scalar)
            scalar.dma_start(g.h[:, :, 0:TOK], xT).then_inc(g.sem["x_in"], 16)
            scalar.dma_start(g.positions, positions).then_inc(g.sem["pos_in"], 16)
            scalar.dma_start(g.h[:, :, TOK:2 * TOK], ctxT).then_inc(g.sem["ctx_in"], 16)
            act.wait_ge(g.sem["tables_in"], act.due("tables_in", 32))
            setup_scalar(act)
            for kind, l in stages:
                PROGRAMS[kind][1](act, l, kind)
                act.chunks += chunk_count(kind)
                act.splits += split_count(kind)

        @block.vector
        def _(vector):
            dve = Engine(g, vector)
            setup_vector(dve)
            dve.wait_ge(g.sem["x_in"], dve.due("x_in", 16))
            dve.wait_ge(g.sem["ctx_in"], dve.due("ctx_in", 16))
            for kind, l in stages:
                PROGRAMS[kind][2](dve, l, kind)
                dve.chunks += chunk_count(kind)
                dve.splits += split_count(kind)
            dve.wait_ge(dve.last_sem, dve.last_count)
            dve.engine.sem_inc(g.sem["all_done"], 1)

        @block.tensor
        def _(tensor):
            pe = Tensor(g, tensor)
            pe.wait_ge(g.sem["tables_in"], pe.due("tables_in", 32))
            for kind, l in stages:
                PROGRAMS[kind][0](pe, l, kind)



def transposed(x):
    return np.ascontiguousarray(x.T.reshape(-1, P, x.shape[0]).transpose(1, 0, 2))


def weight_stream(a, stages):
    total = sum(chunk_count(kind) for kind, _ in stages)
    out = np.zeros((total, P, CHUNK), np.float32)
    n = 0
    for kind, l in stages:
        for chunk in stage_chunks(a, kind, l):
            out[n, :, :chunk.shape[1]] = chunk
            n += 1
    assert n == total
    return out


def laid_out(a, stages=STAGES):
    return {
        "xT": transposed(a["x"][0]),
        "ctxT": transposed(a["ctx_2"][0]),
        "positions": np.ascontiguousarray(np.broadcast_to(a["positions"].astype(np.int32), (P, TOK))),
        "vectors": vector_values(a),
        "consts": constant_values(),
        "weights": weight_stream(a, stages),
    }


def kernel(**inputs):
    import concourse.bacc as bacc
    from concourse.bass_utils import run_bass_kernel_spmd

    a = {name: np.asarray(value) for name, value in inputs.items()}
    arrays = laid_out(a)
    nc = bacc.Bacc("TRN2", target_bir_lowering=False, num_devices=1)
    args = [nc.dram_tensor(name, v.shape, mybir.dt.from_np(v.dtype), kind="ExternalInput").ap()
            for name, v in arrays.items()]
    out = nc.dram_tensor("out", (P, KT, TOK), F32, kind="ExternalOutput").ap()
    program(nc, *args, out)
    r = run_bass_kernel_spmd(nc, [arrays], core_ids=[0])
    got = r.results[0]["out"]
    return np.ascontiguousarray(got.transpose(1, 0, 2).reshape(D, TOK).T).reshape(1, TOK, D)
```
